# Optimizing a Trainium2 kernel written in Bass

```python
import math
import jax, jax.numpy as jnp
from jax import lax
import numpy as np

D_MODEL = 1024
BATCH = 1
SEQ = 512
DEPTH = 2
DEC_BATCH = 8
DEC_SEQ = 4
PAST_LEN = 2048
PAGE_SIZE = 128

N_META = 16
N_ATTN = (DEPTH + 1) // 2
N_SSM = DEPTH // 2
WINDOW = 128
BLOCK = WINDOW
HEAD_DIM = 128
ATTN_WIDTH = 2 * D_MODEL
N_HEADS = ATTN_WIDTH // HEAD_DIM
N_KV_HEADS = 4
GQA_GROUP = N_HEADS // N_KV_HEADS
ATTN_PROJ = ATTN_WIDTH + 2 * N_KV_HEADS * HEAD_DIM + ATTN_WIDTH
D_INNER = 2 * D_MODEL
SSM_HEAD_DIM = 64
SSM_HEADS = D_INNER // SSM_HEAD_DIM
D_STATE = 128
SSM_GROUPS = 4
CONV_W = 4
CONV_DIM = D_INNER + 2 * SSM_GROUPS * D_STATE
SSM_PROJ = D_INNER + CONV_DIM + SSM_HEADS
SSM_CHUNK = 128
EPS = 1e-6

kernel_name = "swa_sink_mamba2_interleaved_step"

def rmsnorm(x, w):
    xf = x.astype(jnp.float32)
    y = xf * lax.rsqrt(jnp.mean(xf * xf, axis=-1, keepdims=True) + EPS)
    return (y * w.astype(jnp.float32)).astype(x.dtype)

def attn_project(u, w_in, q_norm_w, k_norm_w):
    b, L, _ = u.shape
    proj = u @ w_in
    q, k, v, g = jnp.split(proj, [ATTN_WIDTH, ATTN_WIDTH + N_KV_HEADS * HEAD_DIM,
                                  ATTN_WIDTH + 2 * N_KV_HEADS * HEAD_DIM], axis=-1)
    q = rmsnorm(q.reshape(b, L, N_KV_HEADS, GQA_GROUP, HEAD_DIM), q_norm_w)
    k = rmsnorm(k.reshape(b, L, N_KV_HEADS, HEAD_DIM), k_norm_w)
    v = v.reshape(b, L, N_KV_HEADS, HEAD_DIM)
    return q, k, v, g

def attend_with_sink(q, k, v, mask, sinks):
    s = jnp.einsum('...qkgd,...skd->...kgqs', q, k).astype(jnp.float32) * (HEAD_DIM ** -0.5)
    s = jnp.where(mask, s, -jnp.inf)
    sink = sinks.reshape(N_KV_HEADS, GQA_GROUP)[..., None, None].astype(jnp.float32)
    m = jnp.maximum(jnp.max(s, axis=-1, keepdims=True), sink)
    p = jnp.exp(s - m)
    p = p / (jnp.sum(p, axis=-1, keepdims=True) + jnp.exp(sink - m))
    return jnp.einsum('...kgqs,...skd->...qkgd', p.astype(v.dtype), v)

def swa_prompt(u, w_in, q_norm_w, k_norm_w, sinks, w_out):
    b, L, _ = u.shape
    q, k, v, g = attn_project(u, w_in, q_norm_w, k_norm_w)
    pad = (-L) % BLOCK
    Lp = L + pad
    nb = Lp // BLOCK
    qb = jnp.pad(q, ((0, 0), (pad, 0), (0, 0), (0, 0), (0, 0))).reshape(b, nb, BLOCK, N_KV_HEADS, GQA_GROUP, HEAD_DIM)
    kb = jnp.pad(k, ((0, 0), (pad, 0), (0, 0), (0, 0))).reshape(b, nb, BLOCK, N_KV_HEADS, HEAD_DIM)
    vb = jnp.pad(v, ((0, 0), (pad, 0), (0, 0), (0, 0))).reshape(b, nb, BLOCK, N_KV_HEADS, HEAD_DIM)
    shift = ((0, 0), (1, 0), (0, 0), (0, 0), (0, 0))
    keys = jnp.concatenate([jnp.pad(kb[:, :-1], shift), kb], axis=2)
    vals = jnp.concatenate([jnp.pad(vb[:, :-1], shift), vb], axis=2)
    pos = jnp.arange(Lp).reshape(nb, BLOCK) - pad
    kpos = jnp.concatenate([pos - BLOCK, pos], axis=1)
    diff = pos[:, :, None] - kpos[:, None, :]
    mask = (diff >= 0) & (diff < WINDOW) & (kpos[:, None, :] >= 0)
    o = attend_with_sink(qb, keys, vals, mask[None, :, None, None], sinks)
    o = o.reshape(b, Lp, ATTN_WIDTH)[:, pad:]
    out = (o * jax.nn.silu(g)) @ w_out
    return out, k[:, -WINDOW:], v[:, -WINDOW:]

def swa_sample(u, ck, cv, w_in, q_norm_w, k_norm_w, sinks, w_out):
    b, S, _ = u.shape
    q, k, v, g = attn_project(u, w_in, q_norm_w, k_norm_w)
    wbuf = ck.shape[1]
    keys = jnp.concatenate([ck.astype(k.dtype), k], axis=1)
    vals = jnp.concatenate([cv.astype(v.dtype), v], axis=1)
    qpos = jnp.arange(S)
    kpos = jnp.arange(wbuf + S) - wbuf
    diff = qpos[:, None] - kpos[None, :]
    mask = (diff >= 0) & (diff < WINDOW)
    o = attend_with_sink(q, keys, vals, mask[None, None, None], sinks)
    o = o.reshape(b, S, ATTN_WIDTH)
    out = (o * jax.nn.silu(g)) @ w_out
    return out, keys[:, -wbuf:], vals[:, -wbuf:]

def ssd_chunked(x, dt, A, B, C, init_state, chunk):
    f32 = jnp.float32
    b, L, h, p = x.shape
    g, n = B.shape[2], B.shape[3]
    e = h // g
    c = L // chunk
    xg = x.reshape(b, c, chunk, g, e, p).astype(f32)
    dtg = dt.reshape(b, c, chunk, g, e).astype(f32)
    Bg = B.reshape(b, c, chunk, g, n).astype(f32)
    Cg = C.reshape(b, c, chunk, g, n).astype(f32)
    a_cum = jnp.cumsum(dtg * A.reshape(g, e).astype(f32), axis=2)
    xdt = xg * dtg[..., None]
    seg = a_cum[:, :, :, None] - a_cum[:, :, None, :]
    causal = jnp.tril(jnp.ones((chunk, chunk), dtype=bool))[:, :, None, None]
    decay = jnp.exp(jnp.where(causal, seg, -jnp.inf))
    cb = jnp.einsum('bcign,bcjgn->bcijg', Cg, Bg)
    y_diag = jnp.einsum('bcijg,bcijge,bcjgep->bcigep', cb, decay, xdt)
    decay_to_end = jnp.exp(a_cum[:, :, -1:] - a_cum)
    chunk_states = jnp.einsum('bcjgn,bcjge,bcjgep->bcgepn', Bg, decay_to_end, xdt)
    chunk_decay = jnp.exp(a_cum[:, :, -1])

    def step(s, inp):
        st, dec = inp
        return s * dec[..., None, None] + st, s

    init = init_state.reshape(b, g, e, p, n).astype(f32)
    final, starts = lax.scan(step, init, (jnp.moveaxis(chunk_states, 1, 0), jnp.moveaxis(chunk_decay, 1, 0)))
    starts = jnp.moveaxis(starts, 0, 1)
    y_off = jnp.einsum('bcign,bcgepn,bcige->bcigep', Cg, starts, jnp.exp(a_cum))
    y = (y_diag + y_off).reshape(b, L, h, p)
    return y, final.reshape(b, h, p, n)

def mamba2_mixer(u, conv_state, ssm_state, w_in, conv_w, conv_b, dt_bias, a_log, d_skip, norm_w, w_out):
    b, L, _ = u.shape
    proj = u @ w_in
    z, xbc, dt = jnp.split(proj, [D_INNER, D_INNER + CONV_DIM], axis=-1)
    xbc_full = jnp.concatenate([conv_state.astype(xbc.dtype), xbc], axis=1)
    conv = lax.conv_general_dilated(xbc_full, conv_w[:, None, :].astype(xbc.dtype), (1,), 'VALID',
                                    dimension_numbers=('NWC', 'WIO', 'NWC'),
                                    feature_group_count=CONV_DIM)
    xbc_act = jax.nn.silu(conv + conv_b)
    new_conv = xbc_full[:, -(CONV_W - 1):]
    xs, Bm, Cm = jnp.split(xbc_act, [D_INNER, D_INNER + SSM_GROUPS * D_STATE], axis=-1)
    xh = xs.reshape(b, L, SSM_HEADS, SSM_HEAD_DIM)
    Bm = Bm.reshape(b, L, SSM_GROUPS, D_STATE)
    Cm = Cm.reshape(b, L, SSM_GROUPS, D_STATE)
    dtf = jax.nn.softplus(dt.astype(jnp.float32) + dt_bias.astype(jnp.float32))
    A = -jnp.exp(a_log.astype(jnp.float32))
    chunk = min(SSM_CHUNK, L)
    pad = (-L) % chunk
    pad4 = ((0, 0), (pad, 0), (0, 0), (0, 0))
    y, final = ssd_chunked(jnp.pad(xh, pad4), jnp.pad(dtf, ((0, 0), (pad, 0), (0, 0))), A,
                           jnp.pad(Bm, pad4), jnp.pad(Cm, pad4), ssm_state, chunk)
    y = y[:, pad:] + d_skip.astype(jnp.float32)[:, None] * xh.astype(jnp.float32)
    y = y.reshape(b, L, D_INNER) * jax.nn.silu(z.astype(jnp.float32))
    yg = y.reshape(b, L, SSM_GROUPS, D_INNER // SSM_GROUPS)
    yg = yg * lax.rsqrt(jnp.mean(yg * yg, axis=-1, keepdims=True) + EPS)
    y = (yg.reshape(b, L, D_INNER) * norm_w.astype(jnp.float32)).astype(u.dtype)
    return y @ w_out, new_conv, final.astype(u.dtype)

def setup_inputs(seed: int = 0) -> dict:
    key = jax.random.key(seed)
    ks = jax.random.split(key, 24)
    f32 = jnp.float32
    w_buf = min(WINDOW, PAST_LEN)
    nrm = lambda k, shape, s=1.0: jax.random.normal(k, shape, f32) * s
    dt0 = jnp.exp(jax.random.uniform(ks[15], (N_SSM, SSM_HEADS), f32) * (math.log(0.1) - math.log(0.001)) + math.log(0.001))
    return {
        "x_prompt": nrm(ks[0], (BATCH, SEQ, D_MODEL)),
        "x_sample": nrm(ks[1], (DEC_BATCH, DEC_SEQ, D_MODEL)),
        "cache_k": nrm(ks[2], (N_ATTN, DEC_BATCH, w_buf, N_KV_HEADS, HEAD_DIM)),
        "cache_v": nrm(ks[3], (N_ATTN, DEC_BATCH, w_buf, N_KV_HEADS, HEAD_DIM)),
        "state_conv": nrm(ks[4], (N_SSM, DEC_BATCH, CONV_W - 1, CONV_DIM)),
        "state_ssm": nrm(ks[5], (N_SSM, DEC_BATCH, SSM_HEADS, SSM_HEAD_DIM, D_STATE), 0.1),
        "meta_tokens": nrm(ks[6], (N_META, D_MODEL)),
        "norm_w": 1.0 + nrm(ks[7], (DEPTH, D_MODEL), 0.02),
        "w_attn_in": nrm(ks[8], (N_ATTN, D_MODEL, ATTN_PROJ), D_MODEL ** -0.5),
        "q_norm_w": 1.0 + nrm(ks[9], (N_ATTN, HEAD_DIM), 0.02),
        "k_norm_w": 1.0 + nrm(ks[10], (N_ATTN, HEAD_DIM), 0.02),
        "attn_sinks": nrm(ks[11], (N_ATTN, N_HEADS), 0.5),
        "w_attn_out": nrm(ks[12], (N_ATTN, ATTN_WIDTH, D_MODEL), ATTN_WIDTH ** -0.5),
        "w_ssm_in": nrm(ks[13], (N_SSM, D_MODEL, SSM_PROJ), D_MODEL ** -0.5),
        "conv_w": nrm(ks[14], (N_SSM, CONV_W, CONV_DIM), CONV_W ** -0.5),
        "conv_b": nrm(ks[16], (N_SSM, CONV_DIM), 0.01),
        "dt_bias": dt0 + jnp.log(-jnp.expm1(-dt0)),
        "a_log": jnp.log(jax.random.uniform(ks[17], (N_SSM, SSM_HEADS), f32, 1.0, 16.0)),
        "d_skip": 1.0 + nrm(ks[18], (N_SSM, SSM_HEADS), 0.02),
        "ssm_norm_w": 1.0 + nrm(ks[19], (N_SSM, D_INNER), 0.02),
        "w_ssm_out": nrm(ks[20], (N_SSM, D_INNER, D_MODEL), D_INNER ** -0.5),
    }

def reference(x_prompt, x_sample, cache_k, cache_v, state_conv, state_ssm, meta_tokens, norm_w,
              w_attn_in, q_norm_w, k_norm_w, attn_sinks, w_attn_out, w_ssm_in, conv_w, conv_b,
              dt_bias, a_log, d_skip, ssm_norm_w, w_ssm_out):
    bp = x_prompt.shape[0]
    meta = jnp.broadcast_to(meta_tokens[None].astype(x_prompt.dtype), (bp, N_META, D_MODEL))
    xp = jnp.concatenate([meta, x_prompt], axis=1)
    xs = x_sample
    kp_l, vp_l, ks_l, vs_l = [], [], [], []
    cp_l, sp_l, cs_l, ss_l = [], [], [], []
    for i in range(DEPTH):
        j = i // 2
        hp = rmsnorm(xp, norm_w[i])
        hs = rmsnorm(xs, norm_w[i])
        if i % 2 == 0:
            op, kp, vp = swa_prompt(hp, w_attn_in[j], q_norm_w[j], k_norm_w[j], attn_sinks[j], w_attn_out[j])
            os_, ks_, vs_ = swa_sample(hs, cache_k[j], cache_v[j], w_attn_in[j], q_norm_w[j], k_norm_w[j],
                                       attn_sinks[j], w_attn_out[j])
            kp_l.append(kp); vp_l.append(vp); ks_l.append(ks_); vs_l.append(vs_)
        else:
            zc = jnp.zeros((bp, CONV_W - 1, CONV_DIM), xp.dtype)
            zs = jnp.zeros((bp, SSM_HEADS, SSM_HEAD_DIM, D_STATE), jnp.float32)
            op, cp, sp = mamba2_mixer(hp, zc, zs, w_ssm_in[j], conv_w[j], conv_b[j], dt_bias[j], a_log[j],
                                      d_skip[j], ssm_norm_w[j], w_ssm_out[j])
            os_, cs, ss = mamba2_mixer(hs, state_conv[j], state_ssm[j], w_ssm_in[j], conv_w[j], conv_b[j],
                                       dt_bias[j], a_log[j], d_skip[j], ssm_norm_w[j], w_ssm_out[j])
            cp_l.append(cp); sp_l.append(sp); cs_l.append(cs); ss_l.append(ss)
        xp = xp + op
        xs = xs + os_
    y_prompt = xp[:, N_META:]
    y_sample = xs
    return (y_prompt, y_sample,
            jnp.stack(kp_l), jnp.stack(vp_l), jnp.stack(cp_l), jnp.stack(sp_l),
            jnp.stack(ks_l), jnp.stack(vs_l), jnp.stack(cs_l), jnp.stack(ss_l))


_drawn_inputs = setup_inputs


def setup_inputs(seed=0):
    import zlib

    import numpy as np

    out = dict(_drawn_inputs(seed))
    spreads = {}
    factors = {'q_norm_w': 8.0,
     'attn_sinks': 64.0,
     'conv_b': 3.328,
     'd_skip': 15.302,
     'ssm_norm_w': 12.419}
    for name, (base, spread) in spreads.items():
        noise = np.random.default_rng([zlib.crc32(name.encode()), seed]).standard_normal(out[name].shape)
        drawn = base * np.exp(spread * noise) if base else spread * noise
        out[name] = __import__('jax').numpy.asarray(drawn.astype(out[name].dtype))
    for name, factor in factors.items():
        out[name] = (out[name] * factor).astype(out[name].dtype)
    return out
```

```python
from contextlib import ExitStack

import numpy as np
import concourse.bass as bass
from concourse import mybir

F32 = mybir.dt.float32
F32R = mybir.dt.float32r
ACT = mybir.ActivationFunctionType
ALU = mybir.AluOpType

P = 128
D_MODEL, SEQ, N_META, DEC_B, DEC_S = 1024, 512, 16, 8, 4
PROMPT = N_META + SEQ
SAMPLE = DEC_B * DEC_S
T = PROMPT + SAMPLE
HALF = T // 2
GROUPS = 4
HEADS = 4
WIDTH = HEADS * P
SSM_H = 8
KM = D_MODEL // P
XBC = 2048 + 2 * WIDTH
EPS = 1e-6
COL = [0, 16, 144, 272, 400, 528]
LEN = [16, 128, 128, 128, 128, 32]
ORDER = [5, 0, 1, 2, 3, 4]
UNITS = len(ORDER)
STAGES = 2 * GROUPS
HALO = 3
SEG = HALO + DEC_S
CONV_IN = HALO + PROMPT + DEC_B * SEG
CONV_OUT = CONV_IN - HALO
W_SLAB = 2048
RAW_SLOTS, HI_SLOTS, LO_SLOTS = 2, 3, 2
C_ID, C_MASK, C_CAUS, C_SMASK, C_LAST, C_BTOK, C_BEND, C_CB, C_RESET, C_SATT = np.cumsum(
    [0, 128, 256, 128, 32, 32, 8, 8, 256, T]).tolist()
C_END = C_SATT + DEC_B * P + SAMPLE
NEG = -1e30


def shape_constants():
    c = np.zeros((P, C_END), np.float32)
    i, j = np.arange(P)[:, None], np.arange(P)[None, :]
    c[:, C_ID:C_ID + P] = i == j
    k = np.arange(2 * P)[None, :]
    c[:, C_MASK:C_MASK + 2 * P] = np.where((k > i) & (k <= i + P), 0, NEG)
    c[:, C_CAUS:C_CAUS + P] = i <= j
    a, b = np.arange(32)[:, None], np.arange(32)[None, :]
    c[:32, C_SMASK:C_SMASK + 32] = (a <= b) & (a // DEC_S == b // DEC_S)
    c[:32, C_LAST:C_LAST + 32] = a == (b // DEC_S) * DEC_S + DEC_S - 1
    s = np.arange(DEC_B)[None, :]
    c[:32, C_BTOK:C_BTOK + 8] = a // DEC_S == s
    c[:32, C_BEND:C_BEND + 8] = a == s * DEC_S + DEC_S - 1
    c[:, C_CB:C_CB + 256] = (np.arange(DEC_B)[:, None] == np.arange(32)[None, :] // DEC_S).reshape(-1)
    reset = np.ones(T)
    reset[COL[:5]] = 0
    reset[PROMPT::DEC_S] = 0
    c[:, C_RESET:C_RESET + T] = reset
    q = np.arange(P)[:, None] % SAMPLE
    n = np.arange(DEC_B * P)[None, :]
    c[:, C_SATT:C_SATT + DEC_B * P] = np.where((q // DEC_S == n // P) & (n % P > q % DEC_S), 0, NEG)
    m = np.arange(SAMPLE)[None, :]
    c[:, C_SATT + DEC_B * P:] = np.where((q // DEC_S == m // DEC_S) & (m % DEC_S <= q % DEC_S), 0, NEG)
    return c


def plan():
    slabs, halves = [], []

    def add(kind, stage, count, tiles_per_slab):
        for i in range(count):
            slabs.append((kind, stage, i))
            for t in range(tiles_per_slab * i, tiles_per_slab * (i + 1)):
                for half in range(2):
                    halves.append((kind, stage, t, half))

    for s in range(GROUPS):
        add("kv", s, 1, 2)
        if s:
            add("out", s - 1, 2, 4)
        add("q", s, 2, 2)
        add("gate", s, 2, 2)
    add("out", GROUPS - 1, 2, 4)
    add("dt", GROUPS, 1, 1)
    for s in range(GROUPS, STAGES):
        add("bc", s, 1, 2)
        if s > GROUPS:
            add("out", s - 1, 2, 4)
        add("x", s, 2, 2)
        add("z", s, 2, 2)
    add("out", STAGES - 1, 2, 4)
    return slabs, halves


def build(nc, x_prompt, x_sample, cache_k, cache_v, state_conv, state_ssm, meta_tokens, norm_w,
          w_attn_in, q_norm_w, k_norm_w, attn_sinks, w_attn_out, w_ssm_in, conv_w, conv_b, dt_bias,
          a_log, d_skip, ssm_norm_w, w_ssm_out, consts, y_prompt, y_sample, k_prompt, v_prompt,
          conv_prompt, ssm_prompt, k_sample, v_sample, conv_sample, ssm_sample, a_scratch):
    slabs, halves = plan()
    slab_no = {key: n for n, key in enumerate(slabs)}
    half_no = {key: n for n, key in enumerate(halves)}
    n_tiles = {"kv": 2, "out": 8, "q": 4, "gate": 4, "dt": 1, "bc": 2, "x": 4, "z": 4}
    per_slab = {"kv": 2, "out": 4, "q": 2, "gate": 2, "dt": 1, "bc": 2, "x": 2, "z": 2}
    slab_elems = {k: KM * P if k == "dt" else W_SLAB for k in n_tiles}

    def tile_done(kind, stage, tile):
        return half_no[(kind, stage, tile, 1)] + 1

    def slab_done(n):
        kind, stage, i = slabs[n]
        return tile_done(kind, stage, per_slab[kind] * (i + 1) - 1)

    def slab_source(n):
        kind, s, i = slabs[n]
        g = s % GROUPS
        if kind == "out":
            w = w_attn_out if s < GROUPS else w_ssm_out
            v = w[0, g * WIDTH:(g + 1) * WIDTH, i * 512:(i + 1) * 512]
            return [(0, 512, v.rearrange("(k p) n -> p k n", p=P))]
        w = (w_attn_in if s < GROUPS else w_ssm_in)[0].rearrange("(k p) n -> p k n", p=P)
        at = lambda c, n: w[:, :, c:c + n]
        if kind == "kv":
            return [(0, P, at(2048 + g * P, P)), (P, P, at(2560 + g * P, P))]
        if kind == "q":
            return [(0, 256, at(g * WIDTH + i * 256, 256))]
        if kind == "gate":
            return [(0, 256, at(3072 + g * WIDTH + i * 256, 256))]
        if kind == "dt":
            return [(0, 32, at(5120, 32)), (32, 96, at(5024, 96))]
        if kind == "bc":
            return [(0, P, at(4096 + g * P, P)), (P, P, at(4608 + g * P, P))]
        if kind == "x":
            return [(0, 256, at(2048 + g * WIDTH + i * 256, 256))]
        return [(0, 256, at(g * WIDTH + i * 256, 256))]

    raw_count, raw_target = [0] * RAW_SLOTS, []
    for n in range(len(slabs)):
        raw_count[n % RAW_SLOTS] += 16 * len(slab_source(n))
        raw_target.append(raw_count[n % RAW_SLOTS])

    def slab_view(buf, kind):
        k, c = {"out": (4, 512), "dt": (8, P)}.get(kind, (8, 256))
        return buf[:, 0:k * c].rearrange("p (k c) -> p k c", k=k)

    ctx = ExitStack()
    with ctx:
        top = [nc.sbuf_base + -nc.sbuf_base % 32]

        def at(name, shape, dt=F32, offset=None):
            size = int(np.prod(shape[1:])) * 4
            size += -size % 32
            if offset is None:
                offset, top[0] = top[0], top[0] + size
            assert offset + size <= nc.sbuf_usable_end, (name, offset + size)
            where[name] = offset
            return nc.alloc_sbuf_tensor_at(name, shape, dt, offset=offset)

        where = {}
        cst = at("cst", [P, C_END])
        x = at("x", [P, KM, T])
        h_hi = at("h_hi", [P, KM, T], F32R)
        h_lo = at("h_lo", [P, KM, T], F32R)
        rs = at("rs", [P, T])
        raw = [at(f"w_raw{i}_buf", [P, W_SLAB]) for i in range(RAW_SLOTS)]
        w_hi_buf = [at(f"w_hi{i}_buf", [P, W_SLAB], F32R) for i in range(HI_SLOTS)]
        w_lo_buf = [at(f"w_lo{i}_buf", [P, W_SLAB], F32R) for i in range(LO_SLOTS)]
        par = at("par", [P, 154])
        ones = at("ones", [P, P])
        eps = at("eps", [P, 2])
        dskip = at("dskip", [P, 16])
        sinks = at("sinks", [P, 16])
        sink_rows = at("sink_rows", [P, GROUPS])
        dtb = at("dtb", [32, 1])
        alog = at("alog", [32, 1])
        aneg = at("aneg", [32, 1])
        aexp = at("aexp", [32, 1])
        base = top[0]
        q = at("q", [P, HEADS, T])
        gate = at("gate", [P, HEADS, T])
        o = at("o", [P, HEADS, T])
        kn, ksq, rk, kT, kq, vT = (at(n, [P, T]) for n in ("kn", "ksq", "rk", "kT", "kq", "vT"))
        sq = [at(f"sq{i}", [P, T]) for i in range(2)]
        tok = at("tok", [P, 8, P])
        kc = at("kc", [P, DEC_B, P])
        kcT = at("kcT", [P, DEC_B, P])
        vc = at("vc", [P, DEC_B, P])
        sm = [at(f"sm{i}", [P, DEC_B * P + SAMPLE]) for i in range(2)]
        pT = at("pT", [P, 9 * P])
        qs = at("qs", [P, P])
        crow = at("crow", [P, 24])
        mx = at("mx", [P, 2, 8])
        mxc = at("mxc", [P, 8])
        msk = at("msk", [P, 8])
        nm = at("nm", [P, 2, 8])
        ds = at("ds", [P, 2, 8])
        den = at("den", [P, 2, 8])
        es = at("es", [P, 2, 8])
        dsum = at("dsum", [P, 8])
        rden = at("rden", [P, 8])
        og_hi1 = at("og_hi1", [P, HEADS, T], F32R, offset=where["q"])
        og_lo1 = at("og_lo1", [P, HEADS, T], F32R, offset=where["o"])
        end1 = top[0]
        xtok = at("xtok", [P, 6, D_MODEL], offset=where["gate"])
        partok = at("partok", [P, 2, P], offset=where["tok"])
        top[0] = base
        xc = at("xc", [P, HEADS, T])
        z = at("z", [P, HEADS, T])
        y = at("y", [P, HEADS, T])
        bc = at("bc", [P, 2, T])
        rb = [at(f"rb{i}", [P, CONV_IN]) for i in range(2)]
        cv = [at(f"cv{i}", [P, CONV_IN]) for i in range(2)]
        seg = [at(f"seg{i}", [P, SSM_H, P]) for i in range(2)]
        xdt = at("xdt", [P, 2, WIDTH])
        xw = at("xw", [P, 2, WIDTH])
        cbm = at("cbm", [P, 2, P])
        btok = at("btok", [P, 2, P])
        state = at("state", [P, WIDTH])
        ytok = at("ytok", [P, WIDTH])
        s_in = [at(f"s_in{i}", [P, HEADS, P]) for i in range(3)]
        sT = [at(f"sT{i}", [P, WIDTH]) for i in range(2)]
        bmask = at("bmask", [SAMPLE, DEC_B, P])
        cmask = at("cmask", [P, DEC_B, SAMPLE])
        tok2 = at("tok2", [P, 2, 6, 32])
        last = at("last", [P, 3, P])
        ea = at("ea", [P, 6, 32])
        wend = at("wend", [P, 6, 32])
        ealast = at("ealast", [P, 5, 32])
        dec_s = at("dec_s", [P, 16, DEC_B])
        dec_in = at("dec_in", [SAMPLE, 2, 16, DEC_B])
        cn = at("cn", [P, 6, 27])
        y_hi = at("y_hi", [P, HEADS, T], F32R, offset=where["xc"])
        y_lo = at("y_lo", [P, HEADS, T], F32R, offset=where["y"])
        rg = at("rg", [P, T], offset=where["xdt"])
        conv_tok = at("conv_tok", [24, 768], offset=where["seg0"])
        conv_new = at("conv_new", [27, 768], offset=where["seg1"])
        t1, t2, t3, t4 = (at(f"dt_t{i}", [32, T], offset=where["y"] + 4 * T * i) for i in range(4))
        dtT = at("dtT", [32, T], offset=where["z"])
        aT = at("aT", [32, T], offset=where["z"] + 4 * T)
        sqx = [at(f"sqx{i}", [P, T], offset=where[f"sq{i}"]) for i in range(2)]
        yout = [at(f"yout{i}", [P, 5, P], offset=where["bc"] + 2560 * i) for i in range(2)]
        top[0] = max(top[0], end1)

        pp = ctx.enter_context(nc.psum_tensor("pp", [P, 2, 512], F32))
        pS = ctx.enter_context(nc.psum_tensor("pS", [P, 2, 512], F32))
        pT_ = ctx.enter_context(nc.psum_tensor("pT_", [P, 2, 512], F32))
        pO = ctx.enter_context(nc.psum_tensor("pO", [P, 2, 512], F32))
        flat = lambda t: t[:, :, :].rearrange("p a b -> p (a b)")
        fS, fT = flat(pS), flat(pT_)
        misc = pO[:, 1, :]

        def sem(name):
            return ctx.enter_context(nc.semaphore(name))

        s_const, s_par, s_x, s_small = sem("const_in"), sem("par_in"), sem("x_in"), sem("small_in")
        w_raw = [sem(f"w_raw{i}") for i in range(RAW_SLOTS)]
        w_hi, w_lo = sem("w_hi"), sem("w_lo")
        p_done, p_evac = sem("p_done"), sem("p_evac")
        par_tr, par_ready, ones_ready = sem("par_tr"), sem("par_ready"), sem("ones_ready")
        x_tr, x_ready, h_ready = sem("x_tr"), sem("x_ready"), sem("h_ready")
        sqx_ready, ssx_done, rs_ready = sem("sqx_ready"), sem("ssx_done"), sem("rs_ready")
        ksq_ready, kss_done, rk_ready, k_ready = sem("ksq_ready"), sem("kss_done"), sem("rk_ready"), sem("k_ready")
        kc_in, vc_in, kct_tr, kct_ready = sem("kc_in"), sem("vc_in"), sem("kct_tr"), sem("kct_ready")
        tok_tr, tok_ready, kv_out, cache_out = sem("tok_tr"), sem("tok_ready"), sem("kv_out"), sem("cache_out")
        sq_ready, ssq_done, c_ready = sem("sq_ready"), sem("ssq_done"), sem("c_ready")
        s_done, soft_a, exp_done, p_ready = sem("s_done"), sem("soft_a"), sem("exp_done"), sem("p_ready")
        t_done, pt_ready, pv_done, o_ready = sem("t_done"), sem("pt_ready"), sem("pv_done"), sem("o_ready")
        silu_ready, og_ready, og_hi, og_lo = sem("silu_ready"), sem("og_ready"), sem("og_hi"), sem("og_lo")
        dve_step, act_step, pool_step = sem("dve_step"), sem("act_step"), sem("pool_step")
        neg_a, qs_ready = sem("neg_a"), sem("qs_ready")
        dt_e, dt_u, dt_ln, a_ready, a_out = (sem(n) for n in ("dt_e", "dt_u", "dt_ln", "a_ready", "a_out"))
        dt_tr, dt_tok, last_done, last_ready, dec_ready = (sem(n) for n in ("dt_tr", "dt_tok", "last_done", "last_ready", "dec_ready"))
        decin_ready = sem("decin_ready")
        ci_in, hal_tr, conv_done, act_ready = sem("ci_in"), sem("hal_tr"), sem("conv_done"), sem("act_ready")
        cn_tr, cn_new, cn_out = sem("cn_tr"), sem("cn_new"), sem("cn_out")
        e_in = [sem(f"e_in{i}") for i in range(2)]
        clamped = sem("clamped")
        seg_done, l_done, m_done = sem("seg_done"), sem("l_done"), sem("m_done")
        a_done, xw_done, b_done, c_done = sem("a_done"), sem("xw_done"), sem("b_done"), sem("c_done")
        y_done, st_done, d_done = sem("y_done"), sem("st_done"), sem("d_done")
        masks_ready = sem("masks_ready")
        sn_in = [sem(f"sn_in{i}") for i in range(3)]
        sn_out = [sem(f"sn_out{i}") for i in range(3)]
        str_done, sT_ready, sd_done, outer_done, sn_done, yo_done = (
            sem(n) for n in ("str_done", "sT_ready", "sd_done", "outer_done", "sn_done", "yo_done"))
        yz_ready, sqy_ready, ssy_done, rg_ready, yn_ready = (
            sem(n) for n in ("yz_ready", "sqy_ready", "ssy_done", "rg_ready", "yn_ready"))
        fs_tr, fs_ready, fs_out = sem("fs_tr"), sem("fs_ready"), sem("fs_out")
        yt_done, yout_ready = sem("yt_done"), sem("yout_ready")
        y_out = [sem(f"y_out{i}") for i in range(2)]

        ident = cst[:, C_ID:C_ID + P]
        conv_wc = lambda tap, tile: par[:, tap * 24 + tile:tap * 24 + tile + 1]
        conv_bc = lambda tile: par[:, 96 + tile:97 + tile]
        qw, kw = par[:, 120:121], par[:, 121:122]
        norm_c = lambda layer, k: par[:, 122 + layer * 8 + k:123 + layer * 8 + k]
        ssmn_c = lambda tile: par[:, 138 + tile:139 + tile]

        def conv_tile(g, i):
            return [16 + g, 20 + g][i] if i < 2 else 4 * g + i - 2

        def keys_of(c):
            if c == 0:
                return 0, 16, P
            if c == 1:
                return 0, 144, 112
            return COL[c - 1], 2 * P, 0

        def rows_of(c):
            return P if c == 5 else LEN[c]

        def colsum(c):
            return 16 if c == 5 else 17 if c == 0 else (c - 1) * 4

        block = ctx.enter_context(nc.Block())

        @block.sync
        def _(sp):
            sp.dma_start(xtok[0:16, 4, :], meta_tokens).then_inc(s_x, 16)
            for c in range(4):
                sp.dma_start(xtok[:, c, :], x_prompt[0, c * P:(c + 1) * P, :]).then_inc(s_x, 16)
            sp.dma_start(xtok[0:32, 5, :], x_sample.rearrange("b s d -> (b s) d")).then_inc(s_x, 16)
            sp.dma_start(cst[:, :], consts).then_inc(s_const, 16)
            for src, r0, n, j in (
                (conv_w[0].rearrange("k (t c) -> (k t) c", c=P), 0, 96, 0),
                (conv_b.rearrange("a (t c) -> (a t) c", c=P), 96, 24, 0),
                (q_norm_w, 120, 1, 0), (k_norm_w, 121, 1, 0),
                (norm_w.rearrange("l (t c) -> (l t) c", c=P), 0, 16, 1),
                (ssm_norm_w.rearrange("a (t c) -> (a t) c", c=P), 16, 16, 1),
            ):
                sp.dma_start(partok[r0:r0 + n, j, :], src).then_inc(s_par, 16)
            issued = [0]

            def load_slabs(upto):
                while issued[0] < upto:
                    n = issued[0]
                    if n >= RAW_SLOTS:
                        sp.wait_ge(w_hi, n - RAW_SLOTS + 1)
                        sp.wait_ge(w_lo, n - RAW_SLOTS + 1)
                    dst = slab_view(raw[n % RAW_SLOTS], slabs[n][0])
                    for c0, w, src in slab_source(n):
                        sp.dma_start(dst[:, :, c0:c0 + w], src).then_inc(w_raw[n % RAW_SLOTS], 16)
                    issued[0] += 1

            load_slabs(2)
            sp.dma_start(sinks[:, :], attn_sinks[0, :].partition_broadcast(P)).then_inc(s_small, 16)
            for h in range(HEADS):
                src = attn_sinks[0, :].rearrange("(g h) -> h g", h=HEADS)[h]
                sp.dma_start(sink_rows[32 * h:32 * h + 32, :], src.partition_broadcast(32),
                             allow_slow_non_contiguous=True).then_inc(s_small, 16)
            for half in range(2):
                src = d_skip[0, :].rearrange("(t e) -> e t", e=2)[half]
                sp.dma_start(dskip[64 * half:64 * half + 64, :], src.partition_broadcast(64),
                             allow_slow_non_contiguous=True).then_inc(s_small, 16)
            sp.dma_start(dtb[:, :], dt_bias.rearrange("a h -> h a"), allow_slow_non_contiguous=True).then_inc(s_small, 16)
            sp.dma_start(alog[:, :], a_log.rearrange("a h -> h a"), allow_slow_non_contiguous=True).then_inc(s_small, 16)

            def load_cache(g, which):
                dst, src, s = ((kc, cache_k, kc_in), (vc, cache_v, vc_in))[which]
                sp.dma_start(dst[:, :, :], src[0, :, :, g, :].rearrange("b j d -> j b d")).then_inc(s, 16)

            load_cache(0, 0)
            load_cache(0, 1)
            for dst, src in ((k_sample, cache_k), (v_sample, cache_v)):
                sp.dma_start(dst[0, :, 0:P - DEC_S], src[0, :, DEC_S:P]).then_inc(cache_out, 16)
            for s in range(GROUPS):
                load_slabs(slab_no[("gate", s, 1)] + 1)
                sp.wait_ge(tok_ready, s + 1)
                for dst, smp, i in ((v_prompt, v_sample, 3), (k_prompt, k_sample, 6)):
                    sp.dma_start(dst[0, 0, :, s, :], tok[:, i, :]).then_inc(kv_out, 16)
                    j = 5 if i == 3 else 7
                    for b in range(DEC_B):
                        sp.dma_start(smp[0, b, P - DEC_S:P, s, :],
                                     tok[b * DEC_S:(b + 1) * DEC_S, j, :]).then_inc(kv_out, 16)
                if s + 1 < GROUPS:
                    sp.wait_ge(kct_tr, s + 1)
                    load_cache(s + 1, 0)
                load_slabs(slab_no[("gate", s, 1)] + 2)
                if s + 1 < GROUPS:
                    sp.wait_ge(pv_done, UNITS * s + 1)
                    load_cache(s + 1, 1)
            load_slabs(slab_no[("x", GROUPS, 0)] + 1)
            sc = state_conv[0].rearrange("b k c -> (b k) c")

            def final_dst(g):
                return ssm_prompt[0, 0, SSM_H * g:SSM_H * (g + 1)].rearrange("h p n -> (h p) n").rearrange(
                    "(t r) n -> r t n", r=P)

            for g in range(GROUPS):
                s = GROUPS + g
                if g:
                    sp.wait_ge(b_done, UNITS * g)
                else:
                    sp.wait_ge(rs_ready, 2)
                for c0, w, d0 in ((g * WIDTH, WIDTH, 0), (2048 + g * P, P, WIDTH), (2560 + g * P, P, WIDTH + P)):
                    sp.dma_start(conv_tok[:, d0:d0 + w], sc[:, c0:c0 + w]).then_inc(ci_in, 16)
                if g:
                    sp.wait_ge(fs_ready, g)
                    sp.dma_start(final_dst(g - 1), sT[0][:, :].rearrange("p (t n) -> p t n", t=HEADS)).then_inc(fs_out, 16)
                if g == 0:
                    load_slabs(slab_no[("x", s, 1)] + 1)
                    sp.wait_ge(a_ready, 1)
                    sp.dma_start(a_scratch, aT[:, :]).then_inc(a_out, 16)
                load_slabs(slab_no[("z", s, 1)] + 1)
                sp.wait_ge(cn_new, g + 1)
                for c0, w, d0 in ((g * WIDTH, WIDTH, 0), (2048 + g * P, P, WIDTH), (2560 + g * P, P, WIDTH + P)):
                    sp.dma_start(conv_prompt[0, 0, :, c0:c0 + w], conv_new[0:3, d0:d0 + w]).then_inc(cn_out, 16)
                    sp.dma_start(conv_sample[0].rearrange("b k c -> (b k) c")[:, c0:c0 + w],
                                 conv_new[3:27, d0:d0 + w]).then_inc(cn_out, 16)
                load_slabs(slab_no[("z", s, 1)] + 2)
                rows = lambda t, b: t[0, b, SSM_H * g:SSM_H * (g + 1)].rearrange(
                    "h p n -> (h p) n").rearrange("(t r) n -> r t n", r=P)

                def load_state(b):
                    u = DEC_B * g + b
                    if u >= 3:
                        sp.wait_ge(sn_out[u % 3], 16 * (u // 3))
                    sp.dma_start(s_in[u % 3][:, :, :], rows(state_ssm, b)).then_inc(sn_in[u % 3], 16)

                for b in range(2):
                    load_state(b)
                for b in range(DEC_B):
                    u = DEC_B * g + b
                    if b + 2 < DEC_B:
                        load_state(b + 2)
                    sp.wait_ge(sn_done, u + 1)
                    sp.dma_start(rows(ssm_sample, b), s_in[u % 3][:, :, :]).then_inc(sn_out[u % 3], 16)
                if g + 1 < GROUPS:
                    load_slabs(slab_no[("out", s, 0)] + 1)
                else:
                    load_slabs(len(slabs))
            sp.wait_ge(fs_ready, GROUPS)
            sp.dma_start(final_dst(GROUPS - 1), sT[0][:, :].rearrange("p (t n) -> p t n", t=HEADS)).then_inc(fs_out, 16)
            for t in range(KM):
                sp.wait_ge(yout_ready, t + 1)
                sp.dma_start(y_prompt[0].rearrange("(c p) d -> p c d", p=P)[:, :, t * P:(t + 1) * P],
                             yout[t % 2][:, 0:4, :]).then_inc(y_out[t % 2], 16)
                sp.dma_start(y_sample.rearrange("b s d -> (b s) d")[:, t * P:(t + 1) * P],
                             yout[t % 2][0:32, 4, :]).then_inc(y_out[t % 2], 16)
            sp.wait_ge(cache_out, 32)
            sp.wait_ge(kv_out, 16 * 18 * GROUPS)
            sp.wait_ge(a_out, 16)
            sp.wait_ge(cn_out, 96 * GROUPS)
            for i in range(3):
                sp.wait_ge(sn_out[i], 16 * len(range(i, DEC_B * GROUPS, 3)))
            sp.wait_ge(fs_out, 16 * GROUPS)
            for i in range(2):
                sp.wait_ge(y_out[i], 32 * (KM // 2))

        @block.gpsimd
        def _(pool):
            pool.memset(ones[:, :], 1.0).then_inc(ones_ready, 1)
            pool.memset(eps[:, 0:1], EPS).then_inc(ones_ready, 1)
            pool.memset(eps[:, 1:2], EPS * P).then_inc(ones_ready, 1)
            done = [0]

            def split_lo(upto):
                while done[0] < upto:
                    n = done[0]
                    m = slab_elems[slabs[n][0]]
                    pool.wait_ge(w_hi, n + 1)
                    if n >= LO_SLOTS:
                        pool.wait_ge(p_done, slab_done(n - LO_SLOTS))
                    pool.tensor_tensor(w_lo_buf[n % LO_SLOTS][:, 0:m], raw[n % RAW_SLOTS][:, 0:m],
                                       w_hi_buf[n % HI_SLOTS][:, 0:m].bitcast(F32),
                                       ALU.subtract).then_inc(w_lo, 1)
                    done[0] += 1

            for g in range(GROUPS):
                s = GROUPS + g
                split_lo(slab_no[("z", s, 1)])
                for u, c in enumerate(ORDER):
                    v, n = UNITS * g + u, LEN[c]
                    if u == 1:
                        split_lo(slab_no[("z", s, 1)] + 1)
                    if u == 5:
                        split_lo(slab_no[("z", s, 1)] + 2)
                    pool.wait_ge(dt_tok, 3)
                    pool.wait_ge(e_in[v % 2], 16 * (v // 2 + 1))
                    e = seg[v % 2][0:n, :, 0:n]
                    a_j = tok2[0:n, 1, c, SSM_H * g:SSM_H * (g + 1)].unsqueeze(2).to_broadcast([n, SSM_H, n])
                    pool.tensor_tensor(e, e, a_j, ALU.subtract).then_inc(seg_done, 1)
            split_lo(len(slabs))

        @block.scalar
        def _(act):
            done = [0]
            steps = [0]

            def link(ins):
                steps[0] += 1
                ins.then_inc(act_step, 1)
                act.wait_ge(act_step, steps[0])

            def split_hi(count=1):
                for _ in range(count):
                    n = done[0]
                    m = slab_elems[slabs[n][0]]
                    act.wait_ge(w_raw[n % RAW_SLOTS], raw_target[n])
                    if n >= HI_SLOTS:
                        act.wait_ge(p_done, slab_done(n - HI_SLOTS))
                    act.activation(w_hi_buf[n % HI_SLOTS][:, 0:m], raw[n % RAW_SLOTS][:, 0:m],
                                   ACT.Copy).then_inc(w_hi, 1)
                    done[0] += 1

            def exp_tables():
                act.preload_act_table_set("natural_log_exp_and_others")

            exp_tables()
            act.wait_ge(ones_ready, 3)
            act.wait_ge(par_tr, 1)
            act.activation(par[:, 0:122], fT[:, 0:122], ACT.Copy).then_inc(par_ready, 1)
            act.activation(par[:, 122:154], fT[:, 128:160], ACT.Copy).then_inc(par_ready, 1)
            act.wait_ge(s_small, 16 * 9)
            link(act.activation(aexp[:, :], alog[:, :], ACT.Exp))
            act.activation(aneg[:, :], aexp[:, :], ACT.Copy, scale=-1.0).then_inc(neg_a, 1)

            def square_x(layer, k):
                i = layer * KM + k
                act.wait_ge(h_ready, i + 1)
                if i >= 2:
                    act.wait_ge(ssx_done, i - 1)
                act.activation(sqx[i % 2][:, :], x[:, k, :], ACT.Square).then_inc(sqx_ready, 1)

            def norm_scale(layer):
                act.wait_ge(ssx_done, KM * (layer + 1))
                v = rs[:, :].rearrange("p (h t) -> p h t", h=2)
                link(act.activation(v, pO[:, :, 0:HALF], ACT.Ln, bias=eps[:, 0:1], scale=1.0 / D_MODEL))
                act.activation(v, v, ACT.Exp, scale=-0.5).then_inc(rs_ready, 1)

            for k in range(KM):
                act.wait_ge(x_tr, k + 1)
                src = fS if k % 2 == 0 else fT
                act.activation(x[:, k, 0:400], src[:, 0:400], ACT.Copy).then_inc(x_ready, 1)
                act.activation(x[:, k, 400:560], src[:, 512:672], ACT.Copy).then_inc(x_ready, 1)
                if k == 1:
                    split_hi()
                if k:
                    square_x(0, k - 1)
            square_x(0, KM - 1)
            norm_scale(0)

            def square_q(s, h):
                act.wait_ge(p_evac, tile_done("q", s, h))
                if 4 * s + h >= 2:
                    act.wait_ge(ssq_done, 4 * s + h - 1)
                act.activation(sq[h % 2][:, :], q[:, h, :], ACT.Square).then_inc(sq_ready, 1)

            def exps(s, u):
                c, v = ORDER[u], UNITS * s + u
                n, cc = LEN[c], colsum(c)
                act.wait_ge(soft_a, v + 1)
                if c == 5:
                    p = sm[v % 2][:, :]
                    act.activation(p, p, ACT.Exp, bias=nm[:, v % 2, 0:1], scale=crow[:, cc:cc + 1],
                                   accum_out=den[:, v % 2, 0:1])
                    act.activation(es[:, v % 2, 0:1], ds[:, v % 2, 0:1], ACT.Exp).then_inc(exp_done, 1)
                    return
                nk = keys_of(c)[1]
                for h in range(HEADS):
                    p = sm[v % 2][0:n, h * 256:h * 256 + nk]
                    act.activation(p, p, ACT.Exp, bias=nm[0:n, v % 2, h:h + 1], scale=crow[0:n, cc + h:cc + h + 1],
                                   accum_out=den[0:n, v % 2, h:h + 1])
                act.activation(es[0:n, v % 2, 0:4], ds[0:n, v % 2, 0:4], ACT.Exp).then_inc(exp_done, 1)

            def copy_pT(s, u):
                c, v = ORDER[u], UNITS * s + u
                act.wait_ge(t_done, v + 1)
                if v:
                    act.wait_ge(pv_done, v)
                if c == 5:
                    act.activation(pT[:, 0:1024], fT[:, :], ACT.Copy)
                    act.activation(pT[0:32, 1024:1152], misc[0:32, 64:192], ACT.Copy).then_inc(pt_ready, 1)
                elif c == 0:
                    act.activation(pT[0:16, 0:64], fT[0:16, 0:64], ACT.Copy).then_inc(pt_ready, 1)
                elif c == 1:
                    act.activation(pT[0:16, 0:512], fT[0:16, 0:512], ACT.Copy)
                    act.activation(pT[:, 512:1024], fT[:, 512:1024], ACT.Copy).then_inc(pt_ready, 1)
                else:
                    act.activation(pT[:, 0:1024], fT[:, :], ACT.Copy).then_inc(pt_ready, 1)

            def copy_o(s, u):
                c, v = ORDER[u], UNITS * s + u
                n = LEN[c]
                act.wait_ge(pv_done, v + 1)
                if u == 0 and s:
                    act.wait_ge(p_done, tile_done("out", s - 1, 7))
                act.activation(o[:, :, COL[c]:COL[c] + n],
                               pO[:, 0, 0:4 * n].rearrange("p (h n) -> p h n", h=HEADS),
                               ACT.Copy).then_inc(o_ready, 1)

            for s in range(GROUPS):
                if s:
                    split_hi()
                act.wait_ge(p_evac, tile_done("kv", s, 0))
                act.activation(ksq[:, :], kn[:, :], ACT.Square).then_inc(ksq_ready, 1)
                split_hi(1)
                act.wait_ge(kct_tr, s + 1)
                act.activation(kcT[:, :, :].rearrange("p b j -> p (b j)"), fT[:, :], ACT.Copy,
                               scale=qw).then_inc(kct_ready, 1)
                act.wait_ge(kss_done, s + 1)
                v = rk[:, :].rearrange("p (h t) -> p h t", h=2)
                link(act.activation(v, pS[:, :, 0:HALF], ACT.Ln, bias=eps[:, 0:1], scale=1.0 / P))
                act.activation(v, v, ACT.Exp, scale=-0.5).then_inc(rk_ready, 1)
                split_hi()
                square_q(s, 0)
                square_q(s, 1)
                act.wait_ge(tok_tr, s + 1)
                if s:
                    act.wait_ge(kv_out, 16 * 18 * s)
                act.activation(tok[:, 0:4, :].rearrange("p c d -> p (c d)"), fT[:, 0:512], ACT.Copy)
                act.activation(tok[0:16, 4, :], fT[0:16, 512:640], ACT.Copy)
                act.activation(tok[:, 6, :], fT[:, 768:896], ACT.Copy)
                act.activation(tok[0:32, 5, :], fT[0:32, 640:768], ACT.Copy)
                act.activation(tok[0:32, 7, :], fT[0:32, 896:1024], ACT.Copy).then_inc(tok_ready, 1)
                split_hi()
                square_q(s, 2)
                square_q(s, 3)
                split_hi()
                act.wait_ge(ssq_done, 4 * s + 4)
                act.activation(crow[:, 0:17], misc[:, 0:17], ACT.Ln, bias=eps[:, 1:2])
                link(act.activation(crow[0:16, 17:21], misc[0:16, 17:21], ACT.Ln, bias=eps[0:16, 1:2]))
                act.activation(crow[:, 0:17], crow[:, 0:17], ACT.Exp, scale=-0.5)
                act.activation(crow[0:16, 17:21], crow[0:16, 17:21], ACT.Exp, scale=-0.5).then_inc(c_ready, 1)
                exps(s, 0)
                for u in range(1, UNITS):
                    exps(s, u)
                    copy_pT(s, u - 1)
                    copy_o(s, u - 1)
                    if u == 2:
                        split_hi()
                    if u == 5:
                        split_hi()
                copy_pT(s, UNITS - 1)
                copy_o(s, UNITS - 1)
                for h in range(HEADS):
                    act.wait_ge(p_evac, tile_done("gate", s, h))
                    act.activation(gate[:, h, :], gate[:, h, :], ACT.Silu).then_inc(silu_ready, 1)
                act.wait_ge(s_done, UNITS * (s + 1))
                for h in range(HEADS):
                    act.wait_ge(og_ready, 4 * s + h + 1)
                    act.activation(og_hi1[:, h, :], gate[:, h, :], ACT.Copy).then_inc(og_hi, 1)
                exp_tables()

            split_hi()
            for k in range(4):
                square_x(1, k)
            split_hi()
            for k in range(4, 8):
                square_x(1, k)
            split_hi()
            norm_scale(1)
            split_hi()
            act.wait_ge(p_evac, tile_done("dt", GROUPS, 0))
            link(act.activation(t2[:, :], t1[:, :], ACT.Abs))
            act.activation(t2[:, :], t2[:, :], ACT.Exp, scale=-1.0).then_inc(dt_e, 1)
            act.wait_ge(dt_u, 1)
            act.activation(t4[:, :], t3[:, :], ACT.Ln).then_inc(dt_ln, 1)

            def silu_conv(g, i):
                k = 6 * g + i
                act.wait_ge(conv_done, k + 1)
                dst = bc[:, i, :] if i < 2 else xc[:, i - 2, :]
                b = conv_bc(conv_tile(g, i))
                act.activation(dst[:, 0:PROMPT], cv[k % 2][:, 0:PROMPT], ACT.Silu, bias=b)
                act.activation(dst[:, PROMPT:T].rearrange("p (b s) -> p b s", b=DEC_B),
                               cv[k % 2][:, PROMPT + HALO:CONV_IN].rearrange("p (b s) -> p b s", s=SEG)[:, :, 0:DEC_S],
                               ACT.Silu, bias=b).then_inc(act_ready, 1)

            def load_a(v):
                g, c = v // UNITS, ORDER[v % UNITS]
                n = LEN[c]
                if v % UNITS == 0:
                    act.wait_ge(hal_tr, g + 1)
                if v % UNITS == 1:
                    act.wait_ge(cn_out, 96 * (g + 1))
                if v >= 2:
                    act.wait_ge(b_done, v - 1)
                src = a_scratch[SSM_H * g:SSM_H * (g + 1), COL[c]:COL[c] + n]
                act.dma_start(seg[v % 2][0:n, :, 0:n], src.partition_broadcast(n)).then_inc(e_in[v % 2], 16)

            for g in range(GROUPS):
                s = GROUPS + g
                if g:
                    split_hi()
                silu_conv(g, 0)
                silu_conv(g, 1)
                if g:
                    split_hi(2)
                silu_conv(g, 2)
                split_hi()
                silu_conv(g, 3)
                split_hi()
                silu_conv(g, 4)
                silu_conv(g, 5)
                if g == 0:
                    act.wait_ge(a_out, 16)
                load_a(UNITS * g)
                act.wait_ge(cn_tr, g + 1)
                act.activation(conv_new[:, :], fT[0:27, 0:768], ACT.Copy).then_inc(cn_new, 1)
                exp_tables()
                if g == 0:
                    act.wait_ge(last_ready, 1)
                    act.activation(ealast[:, :, :].rearrange("p c h -> p (c h)"),
                                   last[:, 0:2, :].rearrange("p a b -> p (a b)")[:, 0:160], ACT.Exp)
                    act.activation(dec_s[:, :, :].rearrange("p t b -> p (t b)"), last[:, 2, :], ACT.Exp)
                    for n, c0, c1 in ((P, 1, 5), (16, 0, 1), (32, 5, 6)):
                        act.activation(ea[0:n, c0:c1, :], tok2[0:n, 1, c0:c1, :], ACT.Exp)
                        ins = act.activation(wend[0:n, c0:c1, :], wend[0:n, c0:c1, :], ACT.Exp)
                    ins.then_inc(dec_ready, 1)

                def decays(u):
                    c, v = ORDER[u], UNITS * g + u
                    n = LEN[c]
                    act.wait_ge(clamped, v + 1)
                    e = seg[v % 2][0:n, :, 0:n]
                    act.activation(e, e, ACT.Exp).then_inc(l_done, 1)

                decays(0)
                load_a(UNITS * g + 1)
                act.wait_ge(dec_ready, 1)
                for b in range(DEC_B):
                    w = DEC_B * g + b
                    act.wait_ge(str_done, w + 1)
                    if w >= 2:
                        act.wait_ge(yo_done, w - 1)
                    if b == 0 and g:
                        act.wait_ge(fs_out, 16 * g)
                    act.activation(sT[b % 2][:, :], pO[:, b % 2, :], ACT.Copy).then_inc(sT_ready, 1)
                    for t in range(HEADS):
                        i = s_in[w % 3][:, t, :]
                        ins = act.activation(i, i, ACT.Copy, scale=dec_s[:, 4 * g + t, b:b + 1])
                    ins.then_inc(sd_done, 1)
                for u in range(1, UNITS):
                    decays(u)
                    if u + 1 < UNITS:
                        load_a(UNITS * g + u + 1)
                    if u == 2:
                        split_hi()
                    if u == 5:
                        split_hi()
                for t in range(HEADS):
                    act.wait_ge(p_evac, tile_done("z", s, t))
                    act.activation(z[:, t, :], z[:, t, :], ACT.Silu).then_inc(silu_ready, 1)
                for t in range(HEADS):
                    act.wait_ge(yz_ready, 4 * g + t + 1)
                    act.activation(xc[:, t, :], z[:, t, :], ACT.Square).then_inc(sqy_ready, 1)
                exp_tables()
                act.wait_ge(ssy_done, g + 1)
                v = rg[:, :].rearrange("p (h t) -> p h t", h=2)
                link(act.activation(v, pT_[:, :, 0:HALF], ACT.Ln, bias=eps[:, 0:1], scale=1.0 / WIDTH))
                act.activation(v, v, ACT.Exp, scale=-0.5).then_inc(rg_ready, 1)
                for t in range(HEADS):
                    act.wait_ge(yn_ready, 4 * g + t + 1)
                    act.activation(y_hi[:, t, :], z[:, t, :], ACT.Copy).then_inc(og_hi, 1)
                act.wait_ge(fs_tr, g + 1)
                act.activation(sT[0][:, :], pS[:, 1, :], ACT.Copy).then_inc(fs_ready, 1)
            assert done[0] == len(slabs), (done[0], len(slabs))
            for t in range(KM):
                act.wait_ge(yt_done, t + 1)
                if t >= 2:
                    act.wait_ge(y_out[t % 2], 32 * (t // 2))
                src = fS if t % 2 == 0 else fT
                act.activation(yout[t % 2][:, 0:4, :].rearrange("p c d -> p (c d)"), src[:, 0:512], ACT.Copy)
                act.activation(yout[t % 2][0:32, 4, :], src[0:32, 512:640], ACT.Copy).then_inc(yout_ready, 1)

        @block.tensor
        def _(pe):
            def project(kind, s, tile, half):
                j = half_no[(kind, s, tile, half)]
                per = per_slab[kind]
                n = slab_no[(kind, s, tile // per)]
                if tile % per == 0 and half == 0:
                    pe.wait_ge(w_hi, n + 1)
                    pe.wait_ge(w_lo, n + 1)
                if j >= 2:
                    pe.wait_ge(p_evac, j - 1)
                hi = slab_view(w_hi_buf[n % HI_SLOTS], kind)
                lo = slab_view(w_lo_buf[n % LO_SLOTS], kind)
                cols = slice((tile % per) * P, (tile % per + 1) * P)
                tk = slice(half * HALF, (half + 1) * HALF)
                if kind == "out":
                    depth = HEADS
                    a_hi, a_lo = (og_hi1, og_lo1) if s < GROUPS else (y_hi, y_lo)
                else:
                    depth = KM
                    a_hi, a_lo = h_hi, h_lo
                dst = pp[:, j % 2, 0:HALF]
                for k in range(depth):
                    if kind == "out":
                        if tile == 0 and half == 0:
                            pe.wait_ge(og_hi, 4 * s + k + 1)
                            pe.wait_ge(og_lo, 4 * s + k + 1)
                    elif (kind, s) in (("kv", 0), ("dt", GROUPS)) and tile == 0 and half == 0:
                        pe.wait_ge(h_ready, (s // GROUPS) * KM + k + 1)
                    pe.matmul(dst, hi[:, k, cols], a_hi[:, k, tk], start=(k == 0), stop=False)
                    pe.matmul(dst, hi[:, k, cols], a_lo[:, k, tk], start=False, stop=False)
                    mm = pe.matmul(dst, lo[:, k, cols], a_hi[:, k, tk], start=False, stop=(k == depth - 1))
                mm.then_inc(p_done, 1)

            def tile_of(kind, s, tile):
                for half in range(2):
                    project(kind, s, tile, half)

            def sum_x(layer, k):
                i = layer * KM + k
                pe.wait_ge(sqx_ready, i + 1)
                for half in range(2):
                    mm = pe.matmul(pO[:, half, 0:HALF], ones[:, :], sqx[i % 2][:, half * HALF:(half + 1) * HALF],
                                   start=(k == 0), stop=(k == KM - 1))
                mm.then_inc(ssx_done, 1)

            pe.wait_ge(s_const, 16)
            pe.wait_ge(s_par, 96)
            pe.transpose(fT[:, 0:122], partok[0:122, 0, :], ident[0:122, 0:122])
            pe.transpose(fT[:, 128:160], partok[0:32, 1, :], ident[0:32, 0:32]).then_inc(par_tr, 1)
            pe.wait_ge(s_x, 96)
            pe.wait_ge(ones_ready, 3)
            for k in range(KM):
                dst = fS if k % 2 == 0 else fT
                if k == 1:
                    pe.wait_ge(par_ready, 2)
                if k >= 2:
                    pe.wait_ge(x_ready, 2 * (k - 1))
                for c in range(6):
                    n = LEN[c]
                    r = {0: 4, 5: 5}.get(c, c - 1)
                    d0 = COL[c] if c < 4 else COL[c] - 400 + 512
                    mm = pe.transpose(dst[:, d0:d0 + n], xtok[0:n, r, k * P:(k + 1) * P], ident[0:n, 0:n])
                mm.then_inc(x_tr, 1)
                if k >= 2:
                    sum_x(0, k - 2)
            sum_x(0, KM - 2)
            sum_x(0, KM - 1)

            def sum_q(s, h):
                pe.wait_ge(sq_ready, 4 * s + h + 1)
                src = sq[h % 2]
                for c in range(1, 5):
                    pe.matmul(misc[:, colsum(c) + h:colsum(c) + h + 1], src[:, COL[c]:COL[c] + P],
                              ones[:, 0:1], start=True, stop=True)
                pe.matmul(misc[0:16, 17 + h:18 + h], src[:, 0:16], ones[:, 0:1], start=True, stop=True)
                pe.matmul(misc[32 * h:32 * h + 32, 16:17], src[:, PROMPT:T], ones[:, 0:1],
                          start=True, stop=True).then_inc(ssq_done, 1)

            def scores(s, u):
                c, v = ORDER[u], UNITS * s + u
                n = LEN[c]
                if u == 0:
                    pe.wait_ge(k_ready, s + 1)
                    pe.wait_ge(p_evac, tile_done("q", s, 3))
                    pe.wait_ge(kct_ready, s + 1)
                    pe.wait_ge(c_ready, s + 1)
                if v:
                    pe.wait_ge(soft_a, v)
                if c == 5:
                    lhs = qs[:, :]
                    pe.wait_ge(qs_ready, s + 1)
                    for i in range(2):
                        pe.matmul(pS[:, i, :], lhs, kcT[:, 4 * i:4 * i + 4, :], start=True, stop=True)
                    pe.matmul(misc[:, 32:64], lhs, kq[:, PROMPT:T], start=True, stop=True).then_inc(s_done, 1)
                    return
                k0, nk, _ = keys_of(c)
                for h in range(HEADS):
                    mm = pe.matmul(fS[0:n, h * 256:h * 256 + nk], q[:, h, COL[c]:COL[c] + n], kq[:, k0:k0 + nk],
                                   start=True, stop=True)
                mm.then_inc(s_done, 1)

            def transposes(s, u):
                c, v = ORDER[u], UNITS * s + u
                n = LEN[c]
                pe.wait_ge(p_ready, v + 1)
                if v:
                    pe.wait_ge(pt_ready, v)
                if u == 0:
                    pe.wait_ge(tok_ready, s + 1)
                p = sm[v % 2]
                if c == 5:
                    for b in range(DEC_B):
                        pe.transpose(fT[:, b * P:(b + 1) * P], p[:, b * P:(b + 1) * P], ident)
                    mm = pe.transpose(misc[0:32, 64:192], p[:, 1024:1056], ident)
                elif c == 0:
                    for h in range(HEADS):
                        mm = pe.transpose(fT[0:16, h * 16:h * 16 + 16], p[0:16, h * 256:h * 256 + 16], ident[0:16, 0:16])
                else:
                    first = keys_of(c)[1] - P
                    for h in range(HEADS):
                        pe.transpose(fT[0:first, h * P:(h + 1) * P], p[:, h * 256:h * 256 + first], ident)
                        mm = pe.transpose(fT[:, 512 + h * P:512 + (h + 1) * P],
                                          p[:, h * 256 + first:h * 256 + first + P], ident)
                mm.then_inc(t_done, 1)

            def values(s, u):
                c, v = ORDER[u], UNITS * s + u
                pe.wait_ge(pt_ready, v + 1)
                if v:
                    pe.wait_ge(o_ready, v)
                if u == 0:
                    pe.wait_ge(vc_in, 16 * (s + 1))
                if c == 5:
                    dst = pO[:, 0, 0:P]
                    for b in range(DEC_B):
                        pe.matmul(dst, vc[:, b, :], pT[:, b * P:(b + 1) * P], start=(b == 0), stop=False)
                    mm = pe.matmul(dst, tok[0:32, 5, :], pT[0:32, 1024:1152], start=False, stop=True)
                elif c == 0:
                    mm = pe.matmul(pO[:, 0, 0:64], tok[0:16, 4, :], pT[0:16, 0:64], start=True, stop=True)
                else:
                    first = keys_of(c)[1] - P
                    v0 = tok[0:16, 4, :] if c == 1 else tok[:, c - 2, :]
                    pe.matmul(pO[:, 0, :], v0, pT[0:first, 0:512], start=True, stop=False)
                    mm = pe.matmul(pO[:, 0, :], tok[:, c - 1, :], pT[:, 512:1024], start=False, stop=True)
                mm.then_inc(pv_done, 1)

            for s in range(GROUPS):
                tile_of("kv", s, 0)
                tile_of("kv", s, 1)
                if s:
                    for t in range(8):
                        tile_of("out", s - 1, t)
                pe.wait_ge(ksq_ready, s + 1)
                if s:
                    pe.wait_ge(soft_a, UNITS * s)
                else:
                    pe.wait_ge(x_ready, 2 * KM)
                for half in range(2):
                    mm = pe.matmul(pS[:, half, 0:HALF], ones[:, :], ksq[:, half * HALF:(half + 1) * HALF],
                                   start=True, stop=True)
                mm.then_inc(kss_done, 1)
                pe.wait_ge(kc_in, 16 * (s + 1))
                if s:
                    pe.wait_ge(pt_ready, UNITS * s)
                for b in range(DEC_B):
                    mm = pe.transpose(fT[:, b * P:(b + 1) * P], kc[:, b, :], ident)
                mm.then_inc(kct_tr, 1)
                tile_of("q", s, 0)
                tile_of("q", s, 1)
                pe.wait_ge(k_ready, s + 1)
                pe.wait_ge(kct_ready, s + 1)
                for c in range(1, 5):
                    pe.transpose(fT[:, (c - 1) * P:c * P], vT[:, COL[c]:COL[c] + P], ident)
                pe.transpose(fT[0:16, 512:640], vT[:, 0:16], ident)
                pe.transpose(fT[0:32, 640:768], vT[:, PROMPT:T], ident)
                pe.transpose(fT[:, 768:896], kT[:, COL[4]:COL[4] + P], ident)
                pe.transpose(fT[0:32, 896:1024], kT[:, PROMPT:T], ident).then_inc(tok_tr, 1)
                if s == 0:
                    pe.wait_ge(rs_ready, 1)
                sum_q(s, 0)
                tile_of("q", s, 2)
                sum_q(s, 1)
                tile_of("q", s, 3)
                sum_q(s, 2)
                project("gate", s, 0, 0)
                sum_q(s, 3)
                scores(s, 0)
                project("gate", s, 0, 1)
                rest = [(t, half) for t in range(1, 4) for half in range(2)]
                for u in range(1, UNITS):
                    scores(s, u)
                    transposes(s, u - 1)
                    project("gate", s, *rest.pop(0))
                    values(s, u - 1)
                project("gate", s, *rest.pop(0))
                transposes(s, UNITS - 1)
                values(s, UNITS - 1)
            for t in range(8):
                tile_of("out", GROUPS - 1, t)
                if t >= 2:
                    sum_x(1, t - 2)
            sum_x(1, 6)
            sum_x(1, 7)
            tile_of("dt", GROUPS, 0)

            def part_a(g, u):
                c, v = ORDER[u], UNITS * g + u
                n = LEN[c]
                cols = slice(COL[c], COL[c] + n)
                if u == 0:
                    pe.wait_ge(act_ready, 6 * (g + 1))
                    if g:
                        pe.wait_ge(fs_ready, g)
                if v:
                    pe.wait_ge(xw_done, v)
                if u == 1:
                    pe.wait_ge(sn_done, DEC_B * (g + 1))
                pe.matmul(pS[0:n, 0, 0:n], bc[:, 0, cols], bc[:, 1, cols], start=True, stop=True)
                pe.transpose(pS[0:n, 0, P:2 * P], bc[:, 0, cols], ident)
                for t in range(HEADS):
                    mm = pe.transpose(pS[0:n, 1, t * P:(t + 1) * P], xc[:, t, cols], ident)
                mm.then_inc(a_done, 1)

            def part_b(g, u):
                c, v = ORDER[u], UNITS * g + u
                n = LEN[c]
                cols = slice(COL[c], COL[c] + n)
                pe.wait_ge(m_done, v + 1)
                pe.wait_ge(xw_done, v + 1)
                if u == 0:
                    pe.wait_ge(cn_new, g + 1)
                if v:
                    pe.wait_ge(y_done, v)
                if c == 5:
                    pe.wait_ge(masks_ready, g + 1)
                    for b in range(DEC_B + 1):
                        w = DEC_B * g + b
                        if b < DEC_B:
                            pe.wait_ge(sn_in[w % 3], 16 * (w // 3 + 1))
                            if b >= 2:
                                pe.wait_ge(sT_ready, w - 1)
                            elif g == 0:
                                pe.wait_ge(rs_ready, 2)
                            else:
                                pe.wait_ge(d_done, UNITS * g)
                                pe.wait_ge(st_done, 5 * g)
                            for t in range(HEADS):
                                mm = pe.transpose(pO[:, b % 2, t * P:(t + 1) * P], s_in[w % 3][:, t, :], ident)
                            mm.then_inc(str_done, 1)
                            if b >= 2:
                                pe.wait_ge(sn_done, w - 1)
                            for t in range(HEADS):
                                mm = pe.matmul(pS[:, b % 2, t * P:(t + 1) * P], xw[0:n, v % 2, t * P:(t + 1) * P],
                                               bmask[:, b, :], start=True, stop=True)
                            mm.then_inc(outer_done, 1)
                        if b:
                            pe.wait_ge(sT_ready, w)
                            mm = pe.matmul(pT_[0:n, 1, :], cmask[:, b - 1, :], sT[(b - 1) % 2][:, :],
                                           start=(b == 1), stop=(b == DEC_B))
                            mm.then_inc(yo_done, 1)
                for e in range(SSM_H):
                    mm = pe.matmul(pT_[0:n, 0, e * 64:(e + 1) * 64], seg[v % 2][0:n, e, 0:n],
                                   xdt[0:n, v % 2, e * 64:(e + 1) * 64], start=True, stop=True)
                if c == 5:
                    mm.then_inc(b_done, 1)
                    return
                if c:
                    pe.wait_ge(st_done, 5 * g + u - 1)
                    pe.matmul(pT_[0:n, 1, :], bc[:, 1, cols], state[:, :], start=True, stop=True)
                if u == 1:
                    pe.wait_ge(sT_ready, DEC_B * (g + 1))
                pe.matmul(pO[:, 0, :], btok[0:n, v % 2, :], xw[0:n, v % 2, :], start=True, stop=True).then_inc(b_done, 1)

            def part_c(g, u):
                c, v = ORDER[u], UNITS * g + u
                n = LEN[c]
                pe.wait_ge(y_done, v + 1)
                if u == 0:
                    pe.wait_ge(sT_ready, DEC_B * (g + 1))
                if v:
                    pe.wait_ge(d_done, v)
                for t in range(HEADS):
                    mm = pe.transpose(pO[:, 1, t * P:t * P + n], ytok[0:n, t * P:(t + 1) * P], ident[0:n, 0:n])
                mm.then_inc(c_done, 1)

            def sum_y(g):
                for t in range(HEADS):
                    pe.wait_ge(sqy_ready, 4 * g + t + 1)
                    for half in range(2):
                        mm = pe.matmul(pT_[:, half, 0:HALF], ones[:, :], xc[:, t, half * HALF:(half + 1) * HALF],
                                       start=(t == 0), stop=(t == HEADS - 1))
                mm.then_inc(ssy_done, 1)

            def final_state(g):
                pe.wait_ge(st_done, 5 * (g + 1))
                pe.wait_ge(xw_done, UNITS * (g + 1))
                for t in range(HEADS):
                    mm = pe.transpose(pS[:, 1, t * P:(t + 1) * P], state[:, t * P:(t + 1) * P], ident)
                mm.then_inc(fs_tr, 1)

            for g in range(GROUPS):
                s = GROUPS + g
                tile_of("bc", s, 0)
                if g:
                    sum_y(g - 1)
                pe.wait_ge(ci_in, 48 * (g + 1))
                if g:
                    pe.wait_ge(xw_done, UNITS * g)
                else:
                    pe.wait_ge(soft_a, UNITS * GROUPS)
                for i in range(6):
                    mm = pe.transpose(pS[:, 0, i * 24:(i + 1) * 24], conv_tok[:, i * P:(i + 1) * P], ident[0:24, 0:24])
                mm.then_inc(hal_tr, 1)
                tile_of("bc", s, 1)
                if g:
                    final_state(g - 1)
                    for t in range(8):
                        tile_of("out", s - 1, t)
                tile_of("x", s, 0)
                tile_of("x", s, 1)
                if g == 0:
                    pe.wait_ge(a_ready, 1)
                    for i, src in enumerate((dtT, aT)):
                        for c in range(6):
                            mm = pe.transpose(pS[0:LEN[c], 1, i * 192 + c * 32:i * 192 + c * 32 + 32],
                                              src[:, COL[c]:COL[c] + LEN[c]], ident[0:32, 0:32])
                    mm.then_inc(dt_tr, 1)
                tile_of("x", s, 2)
                if g == 0:
                    pe.wait_ge(dt_tok, 3)
                    pe.wait_ge(decin_ready, 1)
                    pe.matmul(pS[:, 1, 0:128], ident[:, P - 1:P].to_broadcast([P, P]),
                              tok2[:, 1, 1:5, :], start=True, stop=True)
                    pe.matmul(pS[:, 1, 128:160], ident[0:16, 15:16].to_broadcast([16, P]),
                              tok2[0:16, 1, 0, :], start=True, stop=True)
                    pe.matmul(pS[0:32, 1, 160:192], cst[0:32, C_LAST:C_LAST + 32], tok2[0:32, 1, 5, :],
                              start=True, stop=True)
                    for i in range(2):
                        mm = pe.matmul(pS[64 * i:64 * i + 64, 1, 256:384], ones[0:32, 0:64],
                                       dec_in[:, i, :, :], start=True, stop=True)
                    mm.then_inc(last_done, 1)
                tile_of("x", s, 3)
                part = [(t, half) for t in range(4) for half in range(2)]
                project("z", s, *part.pop(0))
                pe.wait_ge(conv_done, 6 * (g + 1))
                if g:
                    pe.wait_ge(rg_ready, g)
                else:
                    pe.wait_ge(pt_ready, UNITS * GROUPS)
                for i in range(6):
                    mm = pe.transpose(fT[0:27, i * P:(i + 1) * P], cn[:, i, :], ident)
                mm.then_inc(cn_tr, 1)
                part_a(g, 0)
                part_b(g, 0)
                part_c(g, 0)
                part_a(g, 1)
                project("z", s, *part.pop(0))
                for u in range(2, UNITS):
                    part_a(g, u)
                    part_b(g, u - 1)
                    project("z", s, *part.pop(0))
                    part_c(g, u - 1)
                part_b(g, UNITS - 1)
                project("z", s, *part.pop(0))
                part_c(g, UNITS - 1)
                project("z", s, *part.pop(0))
            sum_y(GROUPS - 1)
            final_state(GROUPS - 1)

            def result(t):
                pe.wait_ge(p_evac, tile_done("out", STAGES - 1, t))
                dst = fS if t % 2 == 0 else fT
                if t == 0:
                    pe.wait_ge(fs_ready, GROUPS)
                if t == 1:
                    pe.wait_ge(rg_ready, GROUPS)
                if t >= 2:
                    pe.wait_ge(yout_ready, t - 1)
                for c in range(1, 5):
                    pe.transpose(dst[:, (c - 1) * P:c * P], x[:, t, COL[c]:COL[c] + P], ident)
                pe.transpose(dst[0:32, 512:640], x[:, t, PROMPT:T], ident).then_inc(yt_done, 1)

            for t in range(8):
                tile_of("out", STAGES - 1, t)
                if t:
                    result(t - 1)
            result(7)

        @block.vector
        def _(dve):
            steps = [0]

            def link(ins):
                steps[0] += 1
                ins.then_inc(dve_step, 1)
                dve.wait_ge(dve_step, steps[0])

            def split_x(layer, k):
                link(dve.tensor_scalar(h_hi[:, k, :], x[:, k, :], norm_c(layer, k), None, ALU.mult))
                dve.scalar_tensor_tensor(h_lo[:, k, :], x[:, k, :], norm_c(layer, k),
                                         h_hi[:, k, :].bitcast(F32), ALU.mult, ALU.subtract).then_inc(h_ready, 1)

            def bank(kind, s, tile, half):
                j = half_no[(kind, s, tile, half)]
                dve.wait_ge(p_done, j + 1)
                return pp[:, j % 2, 0:HALF]

            def scaled(dst, kind, s, tile):
                for half in range(2):
                    tk = slice(half * HALF, (half + 1) * HALF)
                    dve.tensor_tensor(dst[:, tk], bank(kind, s, tile, half), rs[:, tk],
                                      ALU.mult).then_inc(p_evac, 1)

            def add_out(s, tile):
                for half in range(2):
                    tk = slice(half * HALF, (half + 1) * HALF)
                    dve.tensor_tensor(x[:, tile, tk], x[:, tile, tk], bank("out", s, tile, half),
                                      ALU.add).then_inc(p_evac, 1)

            dve.wait_ge(par_ready, 2)
            for k in range(KM):
                dve.wait_ge(x_ready, 2 * (k + 1))
                split_x(0, k)
            dve.wait_ge(rs_ready, 1)

            def soft_max(s, u):
                c, v = ORDER[u], UNITS * s + u
                n, cc, b = rows_of(c), colsum(c), v % 2
                dve.wait_ge(s_done, v + 1)
                dve.wait_ge(c_ready, s + 1)
                if v >= 2:
                    dve.wait_ge(t_done, v - 1)
                if c == 5:
                    dve.tensor_tensor_reduce(sm[b][:, 0:1024], fS, cst[:, C_SATT:C_SATT + 1024], 1.0, 2 * NEG,
                                             ALU.add, ALU.max, mx[:, b, 0:1])
                    link(dve.tensor_tensor_reduce(sm[b][:, 1024:1056], misc[:, 32:64],
                                                  cst[:, C_SATT + 1024:C_SATT + 1056], 1.0, 2 * NEG,
                                                  ALU.add, ALU.max, mx[:, b, 1:2]))
                    w = 1
                    link(dve.tensor_tensor(mx[:, b, 0:1], mx[:, b, 0:1], mx[:, b, 1:2], ALU.max))
                    sink = sink_rows[:, s:s + 1]
                else:
                    _, nk, m0 = keys_of(c)
                    for h in range(HEADS):
                        ins = dve.tensor_tensor_reduce(sm[b][0:n, h * 256:h * 256 + nk], fS[0:n, h * 256:h * 256 + nk],
                                                       cst[0:n, C_MASK + m0:C_MASK + m0 + nk], 1.0, 2 * NEG,
                                                       ALU.add, ALU.max, mx[0:n, b, h:h + 1])
                    link(ins)
                    w = 4
                    sink = sinks[0:n, 4 * s:4 * s + 4]
                link(dve.tensor_tensor(mxc[0:n, 0:w], mx[0:n, b, 0:w], crow[0:n, cc:cc + w], ALU.mult))
                link(dve.tensor_tensor(msk[0:n, 0:w], mxc[0:n, 0:w], sink, ALU.max))
                dve.tensor_scalar(nm[0:n, b, 0:w], msk[0:n, 0:w], -1.0, None, ALU.mult)
                dve.tensor_tensor(ds[0:n, b, 0:w], sink, msk[0:n, 0:w], ALU.subtract).then_inc(soft_a, 1)

            def normalise(s, u):
                c, v = ORDER[u], UNITS * s + u
                n, b = rows_of(c), v % 2
                w = 1 if c == 5 else 4
                dve.wait_ge(exp_done, v + 1)
                link(dve.tensor_tensor(dsum[0:n, 0:w], den[0:n, b, 0:w], es[0:n, b, 0:w], ALU.add))
                link(dve.reciprocal(rden[0:n, 0:w], dsum[0:n, 0:w]))
                for h in range(w):
                    p = sm[b][:, :] if c == 5 else sm[b][0:n, h * 256:h * 256 + keys_of(c)[1]]
                    ins = dve.tensor_scalar(p, p, rden[0:n, h:h + 1], None, ALU.mult)
                ins.then_inc(p_ready, 1)

            dve.wait_ge(s_small, 16 * 9)
            for s in range(GROUPS):
                if s:
                    dve.wait_ge(ksq_ready, s)
                scaled(kn, "kv", s, 0)
                scaled(vT, "kv", s, 1)
                if s:
                    for t in range(8):
                        add_out(s - 1, t)
                dve.wait_ge(rk_ready, s + 1)
                link(dve.scalar_tensor_tensor(kT[:, :], kn[:, :], kw, rk[:, :], ALU.mult, ALU.mult))
                dve.tensor_scalar(kq[:, :], kT[:, :], qw, None, ALU.mult).then_inc(k_ready, 1)
                for h in range(HEADS):
                    scaled(q[:, h, :], "q", s, h)
                dve.wait_ge(p_evac, tile_done("q", s, 3))
                dve.tensor_copy(qs[:, :].rearrange("p (h t) -> p h t", h=HEADS), q[:, :, PROMPT:T]).then_inc(qs_ready, 1)
                rest = [(t, half) for t in range(4) for half in range(2)]

                def evac_gate():
                    t, half = rest.pop(0)
                    tk = slice(half * HALF, (half + 1) * HALF)
                    dve.tensor_tensor(gate[:, t, tk], bank("gate", s, t, half), rs[:, tk],
                                      ALU.mult).then_inc(p_evac, 1)

                if s:
                    dve.wait_ge(og_hi, 4 * s)
                evac_gate()
                soft_max(s, 0)
                evac_gate()
                for u in range(1, UNITS):
                    normalise(s, u - 1)
                    soft_max(s, u)
                    evac_gate()
                evac_gate()
                normalise(s, UNITS - 1)
                dve.wait_ge(o_ready, UNITS * (s + 1))
                for h in range(HEADS + 1):
                    if h < HEADS:
                        dve.wait_ge(silu_ready, 4 * s + h + 1)
                        dve.tensor_tensor(gate[:, h, :], gate[:, h, :], o[:, h, :], ALU.mult).then_inc(og_ready, 1)
                    if h:
                        dve.wait_ge(og_hi, 4 * s + h)
                        dve.wait_ge(og_ready, 4 * s + h)
                        dve.tensor_tensor(og_lo1[:, h - 1, :], gate[:, h - 1, :], og_hi1[:, h - 1, :].bitcast(F32),
                                          ALU.subtract).then_inc(og_lo, 1)
            for t in range(8):
                add_out(GROUPS - 1, t)
                dve.wait_ge(p_evac, tile_done("out", GROUPS - 1, t))
                split_x(1, t)

            dve.wait_ge(rs_ready, 2)
            dve.memset(rb[0][:, 0:HALO], 0.0)
            link(dve.memset(rb[1][:, 0:HALO], 0.0))
            dve.wait_ge(p_done, tile_done("dt", GROUPS, 0))
            for half in range(2):
                tk = slice(half * HALF, (half + 1) * HALF)
                link(dve.tensor_tensor(t1[:, tk], bank("dt", GROUPS, 0, half)[0:32], rs[0:32, tk], ALU.mult))
                dve.tensor_scalar(t1[:, tk], t1[:, tk], dtb[:, :], None, ALU.add).then_inc(p_evac, 1)

            def dt_chain():
                dve.wait_ge(dt_e, 1)
                link(dve.tensor_scalar(t3[:, :], t2[:, :], 1.0, None, ALU.add))
                dve.tensor_scalar(dtT[:, :], t3[:, :], -1.0, None, ALU.add).then_inc(dt_u, 1)
                dve.wait_ge(dt_u, 1)
                link(dve.tensor_tensor(dtT[:, :], t2[:, :], dtT[:, :], ALU.subtract))
                link(dve.reciprocal(aT[:, :], t3[:, :]))
                link(dve.tensor_tensor(dtT[:, :], dtT[:, :], aT[:, :], ALU.mult))
                dve.wait_ge(dt_ln, 1)
                link(dve.tensor_tensor(dtT[:, :], dtT[:, :], t4[:, :], ALU.add))
                link(dve.scalar_tensor_tensor(dtT[:, :], t1[:, :], 0.0, dtT[:, :], ALU.max, ALU.add))
                dve.wait_ge(neg_a, 1)
                link(dve.tensor_scalar(t1[:, :], dtT[:, :], aneg[:, :], None, ALU.mult))
                dve.tensor_tensor_scan(aT[:, :], cst[0:32, C_RESET:C_RESET + T], t1[:, :], 0.0,
                                       ALU.mult, ALU.add).then_inc(a_ready, 1)

            def conv(g, i):
                k = 6 * g + i
                s = GROUPS + g
                r, w = rb[k % 2], cv[k % 2]
                kind, tile = ("bc", i) if i < 2 else ("x", i - 2)
                new = r[:, HALO + PROMPT:CONV_IN].rearrange("p (b s) -> p b s", s=SEG)
                b0 = bank(kind, s, tile, 0)
                dve.tensor_tensor(r[:, HALO:HALO + HALF], b0, rs[:, 0:HALF], ALU.mult).then_inc(p_evac, 1)
                b1 = bank(kind, s, tile, 1)
                m = PROMPT - HALF
                dve.tensor_tensor(r[:, HALO + HALF:HALO + PROMPT], b1[:, 0:m], rs[:, HALF:PROMPT], ALU.mult)
                dve.tensor_tensor(new[:, :, HALO:SEG], b1[:, m:HALF].rearrange("p (b s) -> p b s", b=DEC_B),
                                  rs[:, PROMPT:T].rearrange("p (b s) -> p b s", b=DEC_B),
                                  ALU.mult).then_inc(p_evac, 1)
                dve.wait_ge(hal_tr, g + 1)
                at_ = [4, 5][i] if i < 2 else i - 2
                link(dve.tensor_copy(new[:, :, 0:HALO], pS[:, 0, at_ * 24:(at_ + 1) * 24].rearrange(
                    "p (b s) -> p b s", b=DEC_B)))
                ct = conv_tile(g, i)
                if k >= 2:
                    dve.wait_ge(act_ready, k - 1)
                dve.tensor_copy(cn[:, at_, 0:HALO], r[:, PROMPT:PROMPT + HALO])
                dve.tensor_copy(cn[:, at_, HALO:27].rearrange("p (b s) -> p b s", b=DEC_B), new[:, :, DEC_S:SEG])
                ins = dve.tensor_scalar(w[:, 0:CONV_OUT], r[:, 0:CONV_OUT], conv_wc(0, ct), None, ALU.mult)
                for tap in range(1, 4):
                    link(ins)
                    ins = dve.scalar_tensor_tensor(w[:, 0:CONV_OUT], r[:, tap:tap + CONV_OUT], conv_wc(tap, ct),
                                                   w[:, 0:CONV_OUT], ALU.mult, ALU.add)
                ins.then_inc(conv_done, 1)

            def heads(t, n):
                return t.rearrange("p (e d) -> p e d", e=SSM_H)

            def per_head(t, n, d=64):
                return t.unsqueeze(2).to_broadcast([n, SSM_H, d])

            def prepare(g, u):
                c, v = ORDER[u], UNITS * g + u
                n, b = LEN[c], v % 2
                hs = slice(SSM_H * g, SSM_H * (g + 1))
                dve.wait_ge(a_done, v + 1)
                if v >= 2:
                    dve.wait_ge(b_done, v - 1)
                mask = cst[0:32, C_SMASK:C_SMASK + 32] if c == 5 else cst[0:n, C_CAUS:C_CAUS + n]
                dve.tensor_tensor(cbm[0:n, b, 0:n], pS[0:n, 0, 0:n], mask, ALU.mult)
                dve.tensor_copy(btok[0:n, b, :], pS[0:n, 0, P:2 * P])
                link(dve.tensor_tensor(heads(xdt[0:n, b, :], n), heads(pS[0:n, 1, :], n),
                                       per_head(tok2[0:n, 0, c, hs], n), ALU.mult))
                if v == 0:
                    dve.wait_ge(dec_ready, 1)
                dve.tensor_tensor(heads(xw[0:n, b, :], n), heads(xdt[0:n, b, :], n),
                                  per_head(wend[0:n, c, hs], n), ALU.mult).then_inc(xw_done, 1)
                if c == 5:
                    dve.tensor_tensor(bmask[:, :, :], btok[0:32, b, :].unsqueeze(1).to_broadcast([32, DEC_B, P]),
                                      cst[0:32, C_BTOK:C_BTOK + 8].unsqueeze(2).to_broadcast([32, DEC_B, P]), ALU.mult)
                    dve.tensor_tensor(cmask[:, :, :], bc[:, 1, PROMPT:T].unsqueeze(1).to_broadcast([P, DEC_B, SAMPLE]),
                                      cst[:, C_CB:C_CB + 256].rearrange("p (b s) -> p b s", b=DEC_B),
                                      ALU.mult).then_inc(masks_ready, 1)

            def clamp(g, u):
                v, n = UNITS * g + u, LEN[ORDER[u]]
                dve.wait_ge(seg_done, v + 1)
                e = seg[v % 2][0:n, :, 0:n]
                dve.tensor_scalar(e, e, 0.0, None, ALU.min).then_inc(clamped, 1)

            def mix(g, u):
                c, v = ORDER[u], UNITS * g + u
                n = LEN[c]
                dve.wait_ge(l_done, v + 1)
                dve.wait_ge(xw_done, v + 1)
                e = seg[v % 2][0:n, :, 0:n]
                dve.tensor_tensor(e, e, cbm[0:n, v % 2, 0:n].unsqueeze(1).to_broadcast([n, SSM_H, n]),
                                  ALU.mult).then_inc(m_done, 1)

            def combine(g, u):
                c, v = ORDER[u], UNITS * g + u
                n = LEN[c]
                hs = slice(SSM_H * g, SSM_H * (g + 1))
                dve.wait_ge(b_done, v + 1)
                if v:
                    dve.wait_ge(c_done, v)
                if c == 0:
                    dve.tensor_copy(ytok[0:n, :], pT_[0:n, 0, :]).then_inc(y_done, 1)
                else:
                    link(dve.tensor_tensor(heads(ytok[0:n, :], n), heads(pT_[0:n, 1, :], n),
                                           per_head(ea[0:n, c, hs], n), ALU.mult))
                    dve.tensor_tensor(ytok[0:n, :], ytok[0:n, :], pT_[0:n, 0, :], ALU.add).then_inc(y_done, 1)

            def new_state(g, u):
                c = ORDER[u]
                if c == 5:
                    return
                if c == 0:
                    if g:
                        dve.wait_ge(fs_tr, g)
                    dve.tensor_copy(state[:, :], pO[:, 0, :]).then_inc(st_done, 1)
                    return
                k = c - 1
                link(dve.tensor_tensor(heads(state[:, :], P), heads(state[:, :], P),
                                       per_head(ealast[:, k, SSM_H * g:SSM_H * (g + 1)], P), ALU.mult))
                dve.tensor_tensor(state[:, :], state[:, :], pO[:, 0, :], ALU.add).then_inc(st_done, 1)

            def add_skip(g, u):
                c, v = ORDER[u], UNITS * g + u
                n = LEN[c]
                cols = slice(COL[c], COL[c] + n)
                dve.wait_ge(c_done, v + 1)
                if u == 0 and g:
                    dve.wait_ge(p_done, tile_done("out", GROUPS + g - 1, 7))
                for t in range(HEADS):
                    ins = dve.scalar_tensor_tensor(y[:, t, cols], xc[:, t, cols], dskip[:, 4 * g + t:4 * g + t + 1],
                                                   pO[:, 1, t * P:t * P + n], ALU.mult, ALU.add)
                ins.then_inc(d_done, 1)

            def norm_y(g):
                dve.wait_ge(rg_ready, g + 1)
                for t in range(HEADS):
                    dve.scalar_tensor_tensor(z[:, t, :], z[:, t, :], ssmn_c(4 * g + t), rg[:, :],
                                             ALU.mult, ALU.mult).then_inc(yn_ready, 1)
                dve.wait_ge(yz_ready, 4 * (g + 1))
                for t in range(HEADS):
                    dve.wait_ge(og_hi, 4 * (GROUPS + g) + t + 1)
                    dve.wait_ge(yn_ready, 4 * g + t + 1)
                    dve.tensor_tensor(y_lo[:, t, :], z[:, t, :], y_hi[:, t, :].bitcast(F32),
                                      ALU.subtract).then_inc(og_lo, 1)

            for g in range(GROUPS):
                s = GROUPS + g
                if g:
                    dve.wait_ge(cn_tr, g)
                conv(g, 0)
                if g:
                    norm_y(g - 1)
                conv(g, 1)
                if g:
                    for t in range(8):
                        add_out(s - 1, t)
                else:
                    dt_chain()
                conv(g, 2)
                conv(g, 3)
                if g == 0:
                    dve.wait_ge(dt_tr, 1)
                    for n, c0, c1 in ((P, 1, 5), (16, 0, 1), (32, 5, 6)):
                        dve.tensor_copy(tok2[0:n, :, c0:c1, :], pS[0:n, 1, 0:384].rearrange(
                            "p (a c h) -> p a c h", a=2, c=6)[:, :, c0:c1, :]).then_inc(dt_tok, 1)
                    dve.wait_ge(dt_tok, 3)
                    end = cst[0:32, C_BEND:C_BEND + 8].unsqueeze(1).to_broadcast([32, 16, DEC_B])
                    for i in range(2):
                        a_s = tok2[0:32, 1, 5, :].rearrange("p (t e) -> p e t", e=2)[:, i, :]
                        ins = dve.tensor_tensor(dec_in[:, i, :, :], a_s.unsqueeze(2).to_broadcast([32, 16, DEC_B]),
                                                end, ALU.mult)
                    ins.then_inc(decin_ready, 1)
                conv(g, 4)
                if g == 0:
                    dve.wait_ge(last_done, 1)
                    dve.tensor_copy(last[:, 0:2, :].rearrange("p a b -> p (a b)")[:, 0:160], pS[:, 1, 0:160])
                    dve.tensor_copy(last[0:32, 1, 32:64], pS[0:32, 1, 160:192])
                    link(dve.tensor_copy(last[:, 2, :], pS[:, 1, 256:384]))
                    dve.tensor_tensor(wend[:, 1:5, :], last[:, 0, :].rearrange("p (c h) -> p c h", c=4),
                                      tok2[:, 1, 1:5, :], ALU.subtract)
                    dve.tensor_tensor(wend[0:16, 0, :], last[0:16, 1, 0:32], tok2[0:16, 1, 0, :], ALU.subtract)
                    dve.tensor_tensor(wend[0:32, 5, :], last[0:32, 1, 32:64], tok2[0:32, 1, 5, :],
                                      ALU.subtract).then_inc(last_ready, 1)
                conv(g, 5)
                part = [(t, half) for t in range(4) for half in range(2)]

                def evac_z():
                    t, half = part.pop(0)
                    tk = slice(half * HALF, (half + 1) * HALF)
                    dve.tensor_tensor(z[:, t, tk], bank("z", s, t, half), rs[:, tk], ALU.mult).then_inc(p_evac, 1)

                if g == 0:
                    dve.wait_ge(a_out, 16)
                    dve.wait_ge(dt_tr, 1)
                evac_z()
                clamp(g, 0)
                prepare(g, 0)
                mix(g, 0)
                for b in range(DEC_B):
                    w = DEC_B * g + b
                    dve.wait_ge(outer_done, w + 1)
                    dve.wait_ge(sd_done, w + 1)
                    i = s_in[w % 3][:, :, :].rearrange("p t n -> p (t n)")
                    dve.tensor_tensor(i, i, pS[:, b % 2, :], ALU.add).then_inc(sn_done, 1)
                combine(g, 0)
                add_skip(g, 0)
                clamp(g, 1)
                prepare(g, 1)
                evac_z()
                mix(g, 1)
                for u in range(2, UNITS):
                    prepare(g, u)
                    clamp(g, u)
                    combine(g, u - 1)
                    new_state(g, u - 1)
                    mix(g, u)
                    evac_z()
                    add_skip(g, u - 1)
                combine(g, UNITS - 1)
                new_state(g, UNITS - 1)
                evac_z()
                add_skip(g, UNITS - 1)
                evac_z()
                for t in range(HEADS):
                    dve.wait_ge(silu_ready, 4 * s + t + 1)
                    dve.wait_ge(d_done, UNITS * (g + 1))
                    dve.tensor_tensor(z[:, t, :], z[:, t, :], y[:, t, :], ALU.mult).then_inc(yz_ready, 1)
            norm_y(GROUPS - 1)
            for t in range(8):
                add_out(STAGES - 1, t)


_INS = ["x_prompt", "x_sample", "cache_k", "cache_v", "state_conv", "state_ssm", "meta_tokens", "norm_w",
        "w_attn_in", "q_norm_w", "k_norm_w", "attn_sinks", "w_attn_out", "w_ssm_in", "conv_w", "conv_b",
        "dt_bias", "a_log", "d_skip", "ssm_norm_w", "w_ssm_out"]
_OUTS = [(1, 512, 1024), (8, 4, 1024), (1, 1, 128, 4, 128), (1, 1, 128, 4, 128), (1, 1, 3, 3072),
         (1, 1, 32, 64, 128), (1, 8, 128, 4, 128), (1, 8, 128, 4, 128), (1, 8, 3, 3072), (1, 8, 32, 64, 128)]


def kernel(**inputs):
    import concourse.bacc as bacc
    from concourse.bass_utils import run_bass_kernel_spmd

    nc = bacc.Bacc("TRN2", target_bir_lowering=False, num_devices=1)
    arrays, args = {}, []
    for name in _INS + ["consts"]:
        a = np.ascontiguousarray(shape_constants() if name == "consts" else inputs[name])
        arrays[f"in_{name}"] = a
        args.append(nc.dram_tensor(f"in_{name}", a.shape, mybir.dt.from_np(a.dtype), kind="ExternalInput").ap())
    for i, shape in enumerate(_OUTS):
        args.append(nc.dram_tensor(f"out_{i}", shape, F32, kind="ExternalOutput").ap())
    args.append(nc.dram_tensor("a_scratch", (32, T), F32, kind="Internal").ap())
    build(nc, *args)
    r = run_bass_kernel_spmd(nc, [arrays], core_ids=[0])
    return tuple(r.results[0][f"out_{i}"] for i in range(len(_OUTS)))
```

```python
from contextlib import ExitStack

import numpy as np
import concourse.bass as bass
from concourse import mybir

F32 = mybir.dt.float32
F32R = mybir.dt.float32r
ACT = mybir.ActivationFunctionType
ALU = mybir.AluOpType

P = 128
D_MODEL, SEQ, N_META, DEC_B, DEC_S = 1024, 512, 16, 8, 4
PROMPT = N_META + SEQ
SAMPLE = DEC_B * DEC_S
T = PROMPT + SAMPLE
HALF = T // 2
GROUPS = 4
HEADS = 4
WIDTH = HEADS * P
SSM_H = 8
KM = D_MODEL // P
XBC = 2048 + 2 * WIDTH
EPS = 1e-6
COL = [0, 16, 144, 272, 400, 528]
LEN = [16, 128, 128, 128, 128, 32]
ORDER = [5, 0, 1, 2, 3, 4]
UNITS = len(ORDER)
STAGES = 2 * GROUPS
HALO = 3
SEG = HALO + DEC_S
CONV_IN = HALO + PROMPT + DEC_B * SEG
CONV_OUT = CONV_IN - HALO
W_SLAB = 2048
RAW_SLOTS, HI_SLOTS, LO_SLOTS = 2, 3, 2
STATE_SLOTS = 6
EARLY = COL[4]
STACK = 3 * SAMPLE
C_ID, C_MASK, C_CAUS, C_SMASK, C_LAST, C_BTOK, C_BEND, C_RESET, C_SATT = np.cumsum(
    [0, 128, 256, 128, 32, 32, 8, 8, T]).tolist()
C_END = C_SATT + DEC_B * P + SAMPLE
NEG = -1e30


def shape_constants():
    c = np.zeros((P, C_END), np.float32)
    i, j = np.arange(P)[:, None], np.arange(P)[None, :]
    c[:, C_ID:C_ID + P] = i == j
    k = np.arange(2 * P)[None, :]
    c[:, C_MASK:C_MASK + 2 * P] = np.where((k > i) & (k <= i + P), 0, NEG)
    c[:, C_CAUS:C_CAUS + P] = i <= j
    a, b = np.arange(32)[:, None], np.arange(32)[None, :]
    c[:32, C_SMASK:C_SMASK + 32] = (a <= b) & (a // DEC_S == b // DEC_S)
    c[:32, C_LAST:C_LAST + 32] = a == (b // DEC_S) * DEC_S + DEC_S - 1
    s = np.arange(DEC_B)[None, :]
    c[:STACK, C_BTOK:C_BTOK + 8] = np.tile(a // DEC_S == s, (3, 1))
    c[:32, C_BEND:C_BEND + 8] = a == s * DEC_S + DEC_S - 1
    reset = np.ones(T)
    reset[COL[:5]] = 0
    reset[PROMPT::DEC_S] = 0
    c[:, C_RESET:C_RESET + T] = reset
    q = np.arange(P)[:, None] % SAMPLE
    n = np.arange(DEC_B * P)[None, :]
    c[:, C_SATT:C_SATT + DEC_B * P] = np.where((q // DEC_S == n // P) & (n % P > q % DEC_S), 0, NEG)
    m = np.arange(SAMPLE)[None, :]
    c[:, C_SATT + DEC_B * P:] = np.where((q // DEC_S == m // DEC_S) & (m % DEC_S <= q % DEC_S), 0, NEG)
    return c


def plan():
    slabs, halves = [], []

    def add(kind, stage, count, tiles_per_slab, first=0):
        for i in range(first, first + count):
            slabs.append((kind, stage, i))
            for t in range(tiles_per_slab * i, tiles_per_slab * (i + 1)):
                for half in range(2):
                    halves.append((kind, stage, t, half))

    for s in range(GROUPS):
        add("kv", s, 1, 2)
        if s:
            add("out", s - 1, 2, 4)
        add("q", s, 2, 2)
        add("gate", s, 2, 2)
    add("out", GROUPS - 1, 2, 4)
    add("dt", GROUPS, 1, 1)
    for s in range(GROUPS, STAGES):
        add("bc", s, 1, 2)
        add("x", s, 1, 2)
        if s > GROUPS:
            add("out", s - 1, 2, 4)
        add("x", s, 1, 2, 1)
        add("z", s, 2, 2)
    add("out", STAGES - 1, 2, 4)
    return slabs, halves


def build(nc, x_prompt, x_sample, cache_k, cache_v, state_conv, state_ssm, meta_tokens, norm_w,
          w_attn_in, q_norm_w, k_norm_w, attn_sinks, w_attn_out, w_ssm_in, conv_w, conv_b, dt_bias,
          a_log, d_skip, ssm_norm_w, w_ssm_out, consts, y_prompt, y_sample, k_prompt, v_prompt,
          conv_prompt, ssm_prompt, k_sample, v_sample, conv_sample, ssm_sample, a_scratch):
    slabs, halves = plan()
    slab_no = {key: n for n, key in enumerate(slabs)}
    half_no = {key: n for n, key in enumerate(halves)}
    n_tiles = {"kv": 2, "out": 8, "q": 4, "gate": 4, "dt": 1, "bc": 2, "x": 4, "z": 4}
    per_slab = {"kv": 2, "out": 4, "q": 2, "gate": 2, "dt": 1, "bc": 2, "x": 2, "z": 2}
    slab_elems = {k: KM * P if k == "dt" else W_SLAB for k in n_tiles}

    def tile_done(kind, stage, tile):
        return half_no[(kind, stage, tile, 1)] + 1

    def slab_done(n):
        kind, stage, i = slabs[n]
        return tile_done(kind, stage, per_slab[kind] * (i + 1) - 1)

    def slab_source(n):
        kind, s, i = slabs[n]
        g = s % GROUPS
        if kind == "out":
            w = w_attn_out if s < GROUPS else w_ssm_out
            v = w[0, g * WIDTH:(g + 1) * WIDTH, i * 512:(i + 1) * 512]
            return [(0, 512, v.rearrange("(k p) n -> p k n", p=P))]
        w = (w_attn_in if s < GROUPS else w_ssm_in)[0].rearrange("(k p) n -> p k n", p=P)
        at = lambda c, n: w[:, :, c:c + n]
        if kind == "kv":
            return [(0, P, at(2048 + g * P, P)), (P, P, at(2560 + g * P, P))]
        if kind == "q":
            return [(0, 256, at(g * WIDTH + i * 256, 256))]
        if kind == "gate":
            return [(0, 256, at(3072 + g * WIDTH + i * 256, 256))]
        if kind == "dt":
            return [(0, 32, at(5120, 32)), (32, 96, at(5024, 96))]
        if kind == "bc":
            return [(0, P, at(4096 + g * P, P)), (P, P, at(4608 + g * P, P))]
        if kind == "x":
            return [(0, 256, at(2048 + g * WIDTH + i * 256, 256))]
        return [(0, 256, at(g * WIDTH + i * 256, 256))]

    raw_count, raw_target = [0] * RAW_SLOTS, []
    for n in range(len(slabs)):
        raw_count[n % RAW_SLOTS] += 16 * len(slab_source(n))
        raw_target.append(raw_count[n % RAW_SLOTS])

    def slab_view(buf, kind):
        k, c = {"out": (4, 512), "dt": (8, P)}.get(kind, (8, 256))
        return buf[:, 0:k * c].rearrange("p (k c) -> p k c", k=k)

    ctx = ExitStack()
    with ctx:
        top = [nc.sbuf_base + -nc.sbuf_base % 32]

        def at(name, shape, dt=F32, offset=None):
            size = int(np.prod(shape[1:])) * 4
            size += -size % 32
            if offset is None:
                offset, top[0] = top[0], top[0] + size
            assert offset + size <= nc.sbuf_usable_end, (name, offset + size)
            where[name] = offset
            return nc.alloc_sbuf_tensor_at(name, shape, dt, offset=offset)

        where = {}
        cst = at("cst", [P, C_END])
        x = at("x", [P, KM, T])
        h_hi = at("h_hi", [P, KM, T], F32R)
        h_lo = at("h_lo", [P, KM, T], F32R)
        rs = at("rs", [P, T])
        raw = [at(f"w_raw{i}_buf", [P, W_SLAB]) for i in range(RAW_SLOTS)]
        w_hi_buf = [at(f"w_hi{i}_buf", [P, W_SLAB], F32R) for i in range(HI_SLOTS)]
        w_lo_buf = [at(f"w_lo{i}_buf", [P, W_SLAB], F32R) for i in range(LO_SLOTS)]
        par = at("par", [P, 154])
        ones = at("ones", [P, P])
        eps = at("eps", [P, 2])
        dskip = at("dskip", [P, 16])
        sinks = at("sinks", [P, 16])
        sink_rows = at("sink_rows", [P, GROUPS])
        dtb = at("dtb", [32, 1])
        alog = at("alog", [32, 1])
        aneg = at("aneg", [32, 1])
        aexp = at("aexp", [32, 1])
        base = top[0]
        q = at("q", [P, HEADS, T])
        gate = at("gate", [P, HEADS, T])
        o = at("o", [P, HEADS, T])
        kn, ksq, rk, kT, kq, vT = (at(n, [P, T]) for n in ("kn", "ksq", "rk", "kT", "kq", "vT"))
        sq = [at(f"sq{i}", [P, T]) for i in range(2)]
        tok = at("tok", [P, 8, P])
        kc = at("kc", [P, DEC_B, P])
        kcT = at("kcT", [P, DEC_B, P])
        vc = at("vc", [P, DEC_B, P])
        sm = [at(f"sm{i}", [P, DEC_B * P + SAMPLE]) for i in range(2)]
        pT = at("pT", [P, 9 * P])
        qs = at("qs", [P, P])
        crow = at("crow", [P, 24])
        mx = at("mx", [P, 2, 8])
        mxc = at("mxc", [P, 8])
        msk = at("msk", [P, 8])
        nm = at("nm", [P, 2, 8])
        ds = at("ds", [P, 2, 8])
        den = at("den", [P, 2, 8])
        es = at("es", [P, 2, 8])
        dsum = at("dsum", [P, 8])
        rden = at("rden", [P, 8])
        og_hi1 = at("og_hi1", [P, HEADS, T], F32R, offset=where["q"])
        og_lo1 = at("og_lo1", [P, HEADS, T], F32R, offset=where["o"])
        end1 = top[0]
        xtok = at("xtok", [P, 6, D_MODEL], offset=where["gate"])
        partok = at("partok", [P, 2, P], offset=where["tok"])
        top[0] = base
        xc = at("xc", [P, HEADS, T])
        z = at("z", [P, HEADS, T])
        y = at("y", [P, HEADS, T])
        bc = at("bc", [P, 2, T])
        rb = [at(f"rb{i}", [P, CONV_IN]) for i in range(2)]
        rb.append(at("rb2", [P, CONV_IN], offset=where["cst"] + 4 * C_SATT))
        cv = [at(f"cv{i}", [P, CONV_IN]) for i in range(2)]
        seg = [at(f"seg{i}", [P, SSM_H, P]) for i in range(2)]
        xdt = at("xdt", [P, 2, WIDTH])
        xw = at("xw", [P, 2, WIDTH])
        cbm = at("cbm", [P, 2, P])
        btok = at("btok", [P, 2, P])
        state = at("state", [P, WIDTH])
        ytok = at("ytok", [P, WIDTH])
        s_in = [at(f"s_in{i}", [P, HEADS, P]) for i in range(STATE_SLOTS)]
        sT = [at(f"sT{i}", [P, WIDTH]) for i in range(2)]
        x_parts = at("x_parts", [STACK, WIDTH], F32R, offset=where["rb0"] + 32)
        b_parts = at("b_parts", [STACK, P], F32R, offset=where["rb1"] + 32)
        y_start = at("y_start", [P, HEADS, SAMPLE], offset=where["rb1"] + 32 + 4 * P)
        bmask = at("bmask", [STACK, DEC_B, P], F32R, offset=where["cv0"])
        tok2 = at("tok2", [P, 2, 6, 32])
        last = at("last", [P, 3, P], offset=where["ytok"])
        ea = at("ea", [P, 6, 32])
        wend = at("wend", [P, 6, 32])
        ealast = at("ealast", [P, 5, 32])
        dtw = at("dtw", [SAMPLE, SSM_H])
        dec_s = at("dec_s", [P, 16, DEC_B])
        dec_in = at("dec_in", [SAMPLE, 2, 16, DEC_B], offset=where["sT1"])
        ea_s = at("ea_s", [P, 16, SAMPLE])
        cn = at("cn", [P, 6, 27])
        y_hi = at("y_hi", [P, HEADS, T], F32R, offset=where["xc"])
        y_lo = at("y_lo", [P, HEADS, T], F32R, offset=where["y"])
        rg = at("rg", [P, T], offset=where["xdt"])
        conv_tok = at("conv_tok", [24, 768], offset=where["seg0"])
        conv_new = at("conv_new", [27, 768], offset=where["seg1"])
        t1, t2, t3, t4 = (at(f"dt_t{i}", [32, T], offset=where["y"] + 4 * T * i) for i in range(4))
        dtT = at("dtT", [32, T], offset=where["z"])
        aT = at("aT", [32, T], offset=where["z"] + 4 * T)
        ea_in = at("ea_in", [SAMPLE, 2, 16, SAMPLE], offset=where["z"] + 8 * T)
        xsum = at("xsum", [P, T], offset=where["vT"])
        sqx = [at(f"sqx{i}", [P, T], offset=where[f"sq{i}"]) for i in range(2)]
        yout = [at(f"yout{i}", [P, 5, P], offset=where["bc"] + 2560 * i) for i in range(2)]
        top[0] = max(top[0], end1)

        pp = ctx.enter_context(nc.psum_tensor("pp", [P, 2, 512], F32))
        pS = ctx.enter_context(nc.psum_tensor("pS", [P, 2, 512], F32))
        pT_ = ctx.enter_context(nc.psum_tensor("pT_", [P, 2, 512], F32))
        pO = ctx.enter_context(nc.psum_tensor("pO", [P, 2, 512], F32))
        flat = lambda t: t[:, :, :].rearrange("p a b -> p (a b)")
        fS, fT = flat(pS), flat(pT_)
        misc = pO[:, 1, :]

        def sem(name):
            return ctx.enter_context(nc.semaphore(name))

        s_ident, s_const, s_par, s_small = sem("ident_in"), sem("const_in"), sem("par_in"), sem("small_in")
        s_x = [sem(f"x_in{i}") for i in range(2)]
        w_raw = [sem(f"w_raw{i}") for i in range(RAW_SLOTS)]
        w_hi, w_lo = sem("w_hi"), sem("w_lo")
        p_done, p_evac = sem("p_done"), sem("p_evac")
        par_tr, par_ready, ones_ready = sem("par_tr"), sem("par_ready"), sem("ones_ready")
        x_tr, x_ready, h_ready = sem("x_tr"), sem("x_ready"), sem("h_ready")
        sqx_ready, ssx_done, rs_ready = sem("sqx_ready"), sem("ssx_done"), sem("rs_ready")
        ksq_ready, kss_done, rk_ready, k_ready = sem("ksq_ready"), sem("kss_done"), sem("rk_ready"), sem("k_ready")
        kc_in, vc_in, kct_tr, kct_ready = sem("kc_in"), sem("vc_in"), sem("kct_tr"), sem("kct_ready")
        tok_tr, tok_ready, kv_out, cache_out = sem("tok_tr"), sem("tok_ready"), sem("kv_out"), sem("cache_out")
        sq_ready, ssq_done, c_ready = sem("sq_ready"), sem("ssq_done"), sem("c_ready")
        s_done, soft_a, exp_done, p_ready = sem("s_done"), sem("soft_a"), sem("exp_done"), sem("p_ready")
        t_done, pt_ready, pv_done, o_ready = sem("t_done"), sem("pt_ready"), sem("pv_done"), sem("o_ready")
        silu_ready, og_ready, og_hi, og_lo = sem("silu_ready"), sem("og_ready"), sem("og_hi"), sem("og_lo")
        dve_step, act_step = sem("dve_step"), sem("act_step")
        neg_a, qs_ready = sem("neg_a"), sem("qs_ready")
        dt_e, dt_u, dt_ln, a_ready, a_out = (sem(n) for n in ("dt_e", "dt_u", "dt_ln", "a_ready", "a_out"))
        dt_tr, dt_tok, last_done, last_ready, dec_ready = (sem(n) for n in ("dt_tr", "dt_tok", "last_done", "last_ready", "dec_ready"))
        decin_ready = sem("decin_ready")
        ci_in, hal_tr, conv_done, act_ready = sem("ci_in"), sem("hal_tr"), sem("conv_done"), sem("act_ready")
        cn_tr, cn_new, cn_out = sem("cn_tr"), sem("cn_new"), sem("cn_out")
        e_in = [sem(f"e_in{i}") for i in range(2)]
        clamped, decayed = sem("clamped"), sem("decayed")
        b_ready, bmask_ready = sem("b_ready"), sem("bmask_ready")
        skip_ready = sem("skip_ready")
        sx_ready = sem("sx_ready")
        seg_done, l_done, m_done = sem("seg_done"), sem("l_done"), sem("m_done")
        a_done, xw_done, b_done, c_done = sem("a_done"), sem("xw_done"), sem("b_done"), sem("c_done")
        y_done, st_done, d_done = sem("y_done"), sem("st_done"), sem("d_done")
        sn_in = [sem(f"sn_in{i}") for i in range(STATE_SLOTS)]
        sn_out = [sem(f"sn_out{i}") for i in range(STATE_SLOTS)]
        str_done, sT_ready, outer_done, sn_done, yo_done = (
            sem(n) for n in ("str_done", "sT_ready", "outer_done", "sn_done", "yo_done"))
        yz_ready, sqy_ready, ssy_done, rg_ready, yn_ready = (
            sem(n) for n in ("yz_ready", "sqy_ready", "ssy_done", "rg_ready", "yn_ready"))
        fs_tr, fs_ready, fs_out = sem("fs_tr"), sem("fs_ready"), sem("fs_out")
        yt_done, yout_ready = sem("yt_done"), sem("yout_ready")
        y_out = [sem(f"y_out{i}") for i in range(2)]

        ident = cst[:, C_ID:C_ID + P]
        conv_wc = lambda tap, tile: par[:, tap * 24 + tile:tap * 24 + tile + 1]
        conv_bc = lambda tile: par[:, 96 + tile:97 + tile]
        qw, kw = par[:, 120:121], par[:, 121:122]
        norm_c = lambda layer, k: par[:, 122 + layer * 8 + k:123 + layer * 8 + k]
        ssmn_c = lambda tile: par[:, 138 + tile:139 + tile]

        def conv_tile(g, i):
            return [16 + g, 20 + g][i] if i < 2 else 4 * g + i - 2

        def keys_of(c):
            if c == 0:
                return 0, 16, P
            if c == 1:
                return 0, 144, 112
            return COL[c - 1], 2 * P, 0

        def rows_of(c):
            return P if c == 5 else LEN[c]

        def colsum(c):
            return 16 if c == 5 else 17 if c == 0 else (c - 1) * 4

        def fill_pairs(g):
            return (0, 1, 2) if g + 1 < GROUPS else (0,)

        def part_of(part):
            return slice(EARLY, T) if part else slice(0, EARLY)

        block = ctx.enter_context(nc.Block())

        @block.sync
        def _(sp):
            sp.dma_start(ident, consts[:, C_ID:C_ID + P]).then_inc(s_ident, 16)
            for i in range(2):
                cols = slice(i * D_MODEL // 2, (i + 1) * D_MODEL // 2)
                sp.dma_start(xtok[:, 0:4, cols], x_prompt[0].rearrange("(c p) d -> p c d", p=P)[:, :, cols]).then_inc(s_x[i], 16)
                sp.dma_start(xtok[0:16, 4, cols], meta_tokens[:, cols]).then_inc(s_x[i], 16)
                sp.dma_start(xtok[0:32, 5, cols], x_sample.rearrange("b s d -> (b s) d")[:, cols]).then_inc(s_x[i], 16)
            issued = [0]

            def load_slabs(upto):
                while issued[0] < upto:
                    n = issued[0]
                    if n >= RAW_SLOTS:
                        sp.wait_ge(w_hi, n - RAW_SLOTS + 1)
                        sp.wait_ge(w_lo, n - RAW_SLOTS + 1)
                    dst = slab_view(raw[n % RAW_SLOTS], slabs[n][0])
                    for c0, w, src in slab_source(n):
                        sp.dma_start(dst[:, :, c0:c0 + w], src).then_inc(w_raw[n % RAW_SLOTS], 16)
                    issued[0] += 1

            sp.wait_ge(s_x[0], 48)
            load_slabs(1)
            sp.wait_ge(s_x[1], 48)
            sp.dma_start(cst[:, P:C_END], consts[:, P:C_END]).then_inc(s_const, 16)
            load_slabs(2)
            sp.dma_start(sinks[:, :], attn_sinks[0, :].partition_broadcast(P)).then_inc(s_small, 16)
            for h in range(HEADS):
                src = attn_sinks[0, :].rearrange("(g h) -> h g", h=HEADS)[h]
                sp.dma_start(sink_rows[32 * h:32 * h + 32, :], src.partition_broadcast(32),
                             allow_slow_non_contiguous=True).then_inc(s_small, 16)
            for half in range(2):
                src = d_skip[0, :].rearrange("(t e) -> e t", e=2)[half]
                sp.dma_start(dskip[64 * half:64 * half + 64, :], src.partition_broadcast(64),
                             allow_slow_non_contiguous=True).then_inc(s_small, 16)
            sp.dma_start(dtb[:, :], dt_bias.rearrange("a h -> h a"), allow_slow_non_contiguous=True).then_inc(s_small, 16)
            sp.dma_start(alog[:, :], a_log.rearrange("a h -> h a"), allow_slow_non_contiguous=True).then_inc(s_small, 16)

            def load_cache(g, which):
                dst, src, s = ((kc, cache_k, kc_in), (vc, cache_v, vc_in))[which]
                sp.dma_start(dst[:, :, :], src[0, :, :, g, :].rearrange("b j d -> j b d")).then_inc(s, 16)

            load_cache(0, 0)
            load_cache(0, 1)
            for dst, src in ((k_sample, cache_k), (v_sample, cache_v)):
                sp.dma_start(dst[0, :, 0:P - DEC_S], src[0, :, DEC_S:P]).then_inc(cache_out, 16)
            for s in range(GROUPS):
                load_slabs(slab_no[("gate", s, 1)] + 1)
                sp.wait_ge(tok_ready, s + 1)
                for dst, smp, i in ((v_prompt, v_sample, 3), (k_prompt, k_sample, 6)):
                    sp.dma_start(dst[0, 0, :, s, :], tok[:, i, :]).then_inc(kv_out, 16)
                    j = 5 if i == 3 else 7
                    for b in range(DEC_B):
                        sp.dma_start(smp[0, b, P - DEC_S:P, s, :],
                                     tok[b * DEC_S:(b + 1) * DEC_S, j, :]).then_inc(kv_out, 16)
                if s + 1 < GROUPS:
                    sp.wait_ge(kct_tr, s + 1)
                    load_cache(s + 1, 0)
                load_slabs(slab_no[("gate", s, 1)] + 2)
                if s + 1 < GROUPS:
                    sp.wait_ge(pv_done, UNITS * s + 1)
                    load_cache(s + 1, 1)
            load_slabs(slab_no[("x", GROUPS, 0)] + 1)
            sc = state_conv[0].rearrange("b k c -> (b k) c")

            def final_dst(g):
                return ssm_prompt[0, 0, SSM_H * g:SSM_H * (g + 1)].rearrange("h p n -> (h p) n").rearrange(
                    "(t r) n -> r t n", r=P)

            for g in range(GROUPS):
                s = GROUPS + g
                if g:
                    sp.wait_ge(b_done, UNITS * g - 1)
                else:
                    sp.wait_ge(rs_ready, 2)
                for c0, w, d0 in ((g * WIDTH, WIDTH, 0), (2048 + g * P, P, WIDTH), (2560 + g * P, P, WIDTH + P)):
                    sp.dma_start(conv_tok[:, d0:d0 + w], sc[:, c0:c0 + w]).then_inc(ci_in, 16)
                rows = lambda t, b: t[0, b, SSM_H * g:SSM_H * (g + 1)].rearrange(
                    "h p n -> (h p) n").rearrange("(t r) n -> r t n", r=P)

                def load_state(b):
                    u = DEC_B * g + b
                    if u >= STATE_SLOTS:
                        sp.wait_ge(sn_out[u % STATE_SLOTS], 16 * (u // STATE_SLOTS))
                    sp.dma_start(s_in[u % STATE_SLOTS][:, :, :], rows(state_ssm, b)).then_inc(sn_in[u % STATE_SLOTS], 16)

                for b in range(STATE_SLOTS):
                    load_state(b)
                if g:
                    sp.wait_ge(fs_ready, g)
                    sp.dma_start(final_dst(g - 1), sT[0][:, :].rearrange("p (t n) -> p t n", t=HEADS)).then_inc(fs_out, 16)
                if g == 0:
                    load_slabs(slab_no[("x", s, 1)] + 1)
                    sp.wait_ge(a_ready, 1)
                    sp.dma_start(a_scratch, aT[:, :]).then_inc(a_out, 16)
                load_slabs(slab_no[("z", s, 1)] + 1)
                sp.wait_ge(cn_new, g + 1)
                for c0, w, d0 in ((g * WIDTH, WIDTH, 0), (2048 + g * P, P, WIDTH), (2560 + g * P, P, WIDTH + P)):
                    sp.dma_start(conv_prompt[0, 0, :, c0:c0 + w], conv_new[0:3, d0:d0 + w]).then_inc(cn_out, 16)
                    sp.dma_start(conv_sample[0].rearrange("b k c -> (b k) c")[:, c0:c0 + w],
                                 conv_new[3:27, d0:d0 + w]).then_inc(cn_out, 16)
                load_slabs(slab_no[("z", s, 1)] + 2)
                for b in range(DEC_B):
                    u = DEC_B * g + b
                    sp.wait_ge(sn_done, DEC_B * g + 2 * (b // 2 + 1))
                    sp.dma_start(rows(ssm_sample, b), s_in[u % STATE_SLOTS][:, :, :]).then_inc(sn_out[u % STATE_SLOTS], 16)
                    if b + STATE_SLOTS < DEC_B:
                        load_state(b + STATE_SLOTS)
                load_slabs(min(slab_no[("z", s, 1)] + 4, len(slabs)))
            sp.wait_ge(fs_ready, GROUPS)
            sp.dma_start(final_dst(GROUPS - 1), sT[0][:, :].rearrange("p (t n) -> p t n", t=HEADS)).then_inc(fs_out, 16)
            for t in range(KM):
                sp.wait_ge(yout_ready, t + 1)
                sp.dma_start(y_prompt[0].rearrange("(c p) d -> p c d", p=P)[:, :, t * P:(t + 1) * P],
                             yout[t % 2][:, 0:4, :]).then_inc(y_out[t % 2], 16)
                sp.dma_start(y_sample.rearrange("b s d -> (b s) d")[:, t * P:(t + 1) * P],
                             yout[t % 2][0:32, 4, :]).then_inc(y_out[t % 2], 16)
            sp.wait_ge(cache_out, 32)
            sp.wait_ge(kv_out, 16 * 18 * GROUPS)
            sp.wait_ge(a_out, 16)
            sp.wait_ge(cn_out, 96 * GROUPS)
            for i in range(STATE_SLOTS):
                sp.wait_ge(sn_out[i], 16 * len(range(i, DEC_B * GROUPS, STATE_SLOTS)))
            sp.wait_ge(fs_out, 16 * GROUPS)
            for i in range(2):
                sp.wait_ge(y_out[i], 32 * (KM // 2))

        @block.gpsimd
        def _(pool):
            pool.memset(ones[:, :], 1.0).then_inc(ones_ready, 1)
            pool.memset(eps[:, 0:1], EPS).then_inc(ones_ready, 1)
            pool.memset(eps[:, 1:2], EPS * P).then_inc(ones_ready, 1)
            done = [0]

            def split_lo(upto):
                while done[0] < upto:
                    n = done[0]
                    m = slab_elems[slabs[n][0]]
                    pool.wait_ge(w_hi, n + 1)
                    if n >= LO_SLOTS:
                        pool.wait_ge(p_done, slab_done(n - LO_SLOTS))
                    pool.tensor_tensor(w_lo_buf[n % LO_SLOTS][:, 0:m], raw[n % RAW_SLOTS][:, 0:m],
                                       w_hi_buf[n % HI_SLOTS][:, 0:m].bitcast(F32),
                                       ALU.subtract).then_inc(w_lo, 1)
                    done[0] += 1

            def decay_state(g, u):
                if u >= 2:
                    pool.wait_ge(b_done, UNITS * g + u + 1)
                    pool.wait_ge(st_done, 5 * g + u - 1)
                    k = ORDER[u] - 1
                    st = state[:, :].rearrange("p (e d) -> p e d", e=SSM_H)
                    by = ealast[:, k, SSM_H * g:SSM_H * (g + 1)].unsqueeze(2).to_broadcast([P, SSM_H, 64])
                    pool.tensor_tensor(st, st, by, ALU.mult).then_inc(decayed, 1)

            split_lo(slab_no[("out", GROUPS - 1, 1)] + 1)
            for k in range(1, KM - 2):
                pool.wait_ge(sqx_ready, KM + k + 1)
                if k > 1:
                    pool.wait_ge(sx_ready, k - 1)
                first = sqx[0] if k == 1 else xsum
                pool.tensor_tensor(xsum[:, :], first[:, :], sqx[k % 2][:, :], ALU.add).then_inc(sx_ready, 1)
                if k == 5:
                    split_lo(slab_no[("dt", GROUPS, 0)] + 1)
            for g in range(GROUPS):
                s = GROUPS + g
                split_lo(slab_no[("z", s, 1)] + 1)
                for u, c in enumerate(ORDER):
                    v, n = UNITS * g + u, LEN[c]
                    if u == (2 if g + 1 < GROUPS else 5):
                        split_lo(slab_no[("z", s, 1)] + 2)
                    pool.wait_ge(dt_tok, 3)
                    pool.wait_ge(e_in[v % 2], 16 * (v // 2 + 1))
                    e = seg[v % 2][0:n, :, 0:n]
                    a_j = tok2[0:n, 1, c, SSM_H * g:SSM_H * (g + 1)].unsqueeze(2).to_broadcast([n, SSM_H, n])
                    pool.tensor_tensor(e, e, a_j, ALU.subtract).then_inc(seg_done, 1)
                    decay_state(g, u - 1)
                    if u == 4 and g + 1 < GROUPS:
                        split_lo(slab_no[("z", s, 1)] + 3)
                decay_state(g, UNITS - 1)
            split_lo(len(slabs))

        @block.scalar
        def _(act):
            done = [0]
            steps = [0]

            def link(ins):
                steps[0] += 1
                ins.then_inc(act_step, 1)
                act.wait_ge(act_step, steps[0])

            def split_hi(count=1):
                for _ in range(count):
                    n = done[0]
                    m = slab_elems[slabs[n][0]]
                    act.wait_ge(w_raw[n % RAW_SLOTS], raw_target[n])
                    if n >= HI_SLOTS:
                        act.wait_ge(p_done, slab_done(n - HI_SLOTS))
                    act.activation(w_hi_buf[n % HI_SLOTS][:, 0:m], raw[n % RAW_SLOTS][:, 0:m],
                                   ACT.Copy).then_inc(w_hi, 1)
                    done[0] += 1

            def exp_tables():
                act.preload_act_table_set("natural_log_exp_and_others")

            exp_tables()
            for src, r0, n, j in (
                (conv_w[0].rearrange("k (t c) -> (k t) c", c=P), 0, 96, 0),
                (conv_b.rearrange("a (t c) -> (a t) c", c=P), 96, 24, 0),
                (q_norm_w, 120, 1, 0), (k_norm_w, 121, 1, 0),
                (norm_w.rearrange("l (t c) -> (l t) c", c=P), 0, 16, 1),
                (ssm_norm_w.rearrange("a (t c) -> (a t) c", c=P), 16, 16, 1),
            ):
                act.dma_start(partok[r0:r0 + n, j, :], src).then_inc(s_par, 16)
            act.wait_ge(ones_ready, 3)

            def square_x(layer, k):
                i = layer * KM + k
                act.wait_ge(h_ready, i + 1)
                if layer and k >= 2:
                    act.wait_ge(sx_ready, max(k - 2, 1))
                elif layer == 0 and k >= 2:
                    act.wait_ge(ssx_done, k - 1)
                act.activation(sqx[i % 2][:, :], x[:, k, :], ACT.Square).then_inc(sqx_ready, 1)

            def norm_scale(layer):
                act.wait_ge(ssx_done, KM + layer)
                v = rs[:, :].rearrange("p (h t) -> p h t", h=2)
                link(act.activation(v, pO[:, :, 0:HALF], ACT.Ln, bias=eps[:, 0:1], scale=1.0 / D_MODEL))
                act.activation(v, v, ACT.Exp, scale=-0.5).then_inc(rs_ready, 1)

            for k in range(KM):
                act.wait_ge(x_tr, k + 1)
                src = fS if k % 2 == 0 else fT
                act.activation(x[:, k, 0:400], src[:, 0:400], ACT.Copy).then_inc(x_ready, 1)
                act.activation(x[:, k, 400:560], src[:, 512:672], ACT.Copy).then_inc(x_ready, 1)
                if k == 1:
                    act.wait_ge(par_tr, 1)
                    act.activation(par[:, 0:122], misc[:, 0:122], ACT.Copy).then_inc(par_ready, 1)
                    act.activation(par[:, 122:154], misc[:, 128:160], ACT.Copy).then_inc(par_ready, 1)
                if k == 3:
                    split_hi()
                if k:
                    square_x(0, k - 1)
            square_x(0, KM - 1)
            norm_scale(0)
            act.wait_ge(s_small, 16 * 9)
            link(act.activation(aexp[:, :], alog[:, :], ACT.Exp))
            act.activation(aneg[:, :], aexp[:, :], ACT.Copy, scale=-1.0).then_inc(neg_a, 1)

            def square_q(s, h):
                act.wait_ge(p_evac, tile_done("q", s, h))
                if 4 * s + h >= 2:
                    act.wait_ge(ssq_done, 4 * s + h - 1)
                act.activation(sq[h % 2][:, :], q[:, h, :], ACT.Square).then_inc(sq_ready, 1)

            def exps(s, u):
                c, v = ORDER[u], UNITS * s + u
                n, cc = LEN[c], colsum(c)
                act.wait_ge(soft_a, v + 1)
                if c == 5:
                    p = sm[v % 2][:, :]
                    act.activation(p, p, ACT.Exp, bias=nm[:, v % 2, 0:1], scale=crow[:, cc:cc + 1],
                                   accum_out=den[:, v % 2, 0:1])
                    act.activation(es[:, v % 2, 0:1], ds[:, v % 2, 0:1], ACT.Exp).then_inc(exp_done, 1)
                    return
                nk = keys_of(c)[1]
                for h in range(HEADS):
                    p = sm[v % 2][0:n, h * 256:h * 256 + nk]
                    act.activation(p, p, ACT.Exp, bias=nm[0:n, v % 2, h:h + 1], scale=crow[0:n, cc + h:cc + h + 1],
                                   accum_out=den[0:n, v % 2, h:h + 1])
                act.activation(es[0:n, v % 2, 0:4], ds[0:n, v % 2, 0:4], ACT.Exp).then_inc(exp_done, 1)

            def copy_pT(s, u):
                c, v = ORDER[u], UNITS * s + u
                act.wait_ge(t_done, v + 1)
                if v:
                    act.wait_ge(pv_done, v)
                if c == 5:
                    act.activation(pT[:, 0:1024], fT[:, :], ACT.Copy)
                    act.activation(pT[0:32, 1024:1152], misc[0:32, 64:192], ACT.Copy).then_inc(pt_ready, 1)
                elif c == 0:
                    act.activation(pT[0:16, 0:64], fT[0:16, 0:64], ACT.Copy).then_inc(pt_ready, 1)
                elif c == 1:
                    act.activation(pT[0:16, 0:512], fT[0:16, 0:512], ACT.Copy)
                    act.activation(pT[:, 512:1024], fT[:, 512:1024], ACT.Copy).then_inc(pt_ready, 1)
                else:
                    act.activation(pT[:, 0:1024], fT[:, :], ACT.Copy).then_inc(pt_ready, 1)

            def copy_o(s, u):
                c, v = ORDER[u], UNITS * s + u
                n = LEN[c]
                act.wait_ge(pv_done, v + 1)
                if u == 0 and s:
                    act.wait_ge(p_done, tile_done("out", s - 1, 7))
                act.activation(o[:, :, COL[c]:COL[c] + n],
                               pO[:, 0, 0:4 * n].rearrange("p (h n) -> p h n", h=HEADS),
                               ACT.Copy).then_inc(o_ready, 1)

            for s in range(GROUPS):
                if s:
                    split_hi()
                act.wait_ge(p_evac, tile_done("kv", s, 0))
                act.activation(ksq[:, :], kn[:, :], ACT.Square).then_inc(ksq_ready, 1)
                split_hi(1)
                act.wait_ge(kct_tr, s + 1)
                act.activation(kcT[:, :, :].rearrange("p b j -> p (b j)"), fT[:, :], ACT.Copy,
                               scale=qw).then_inc(kct_ready, 1)
                act.wait_ge(kss_done, s + 1)
                v = rk[:, :].rearrange("p (h t) -> p h t", h=2)
                link(act.activation(v, pS[:, :, 0:HALF], ACT.Ln, bias=eps[:, 0:1], scale=1.0 / P))
                act.activation(v, v, ACT.Exp, scale=-0.5).then_inc(rk_ready, 1)
                split_hi()
                square_q(s, 0)
                square_q(s, 1)
                act.wait_ge(tok_tr, s + 1)
                if s:
                    act.wait_ge(kv_out, 16 * 18 * s)
                act.activation(tok[:, 0:4, :].rearrange("p c d -> p (c d)"), fT[:, 0:512], ACT.Copy)
                act.activation(tok[0:16, 4, :], fT[0:16, 512:640], ACT.Copy)
                act.activation(tok[:, 6, :], fT[:, 768:896], ACT.Copy)
                act.activation(tok[0:32, 5, :], fT[0:32, 640:768], ACT.Copy)
                act.activation(tok[0:32, 7, :], fT[0:32, 896:1024], ACT.Copy).then_inc(tok_ready, 1)
                split_hi()
                square_q(s, 2)
                square_q(s, 3)
                split_hi()
                act.wait_ge(ssq_done, 4 * s + 4)
                act.activation(crow[:, 0:17], misc[:, 0:17], ACT.Ln, bias=eps[:, 1:2])
                link(act.activation(crow[0:16, 17:21], misc[0:16, 17:21], ACT.Ln, bias=eps[0:16, 1:2]))
                act.activation(crow[:, 0:17], crow[:, 0:17], ACT.Exp, scale=-0.5)
                act.activation(crow[0:16, 17:21], crow[0:16, 17:21], ACT.Exp, scale=-0.5).then_inc(c_ready, 1)
                exps(s, 0)
                for u in range(1, UNITS):
                    copy_pT(s, u - 1)
                    exps(s, u)
                    copy_o(s, u - 1)
                    if u == 2:
                        split_hi()
                    if u == 5:
                        split_hi()
                for h in range(HEADS):
                    if h == (2 if s + 1 < GROUPS else 0):
                        copy_pT(s, UNITS - 1)
                    act.wait_ge(p_evac, tile_done("gate", s, h))
                    act.activation(gate[:, h, :], gate[:, h, :], ACT.Silu).then_inc(silu_ready, 1)
                copy_o(s, UNITS - 1)
                act.wait_ge(s_done, UNITS * (s + 1))
                for h in range(HEADS):
                    act.wait_ge(og_ready, 4 * s + h + 1)
                    act.activation(og_hi1[:, h, :], gate[:, h, :], ACT.Copy).then_inc(og_hi, 1)
                exp_tables()

            split_hi()
            for k in range(4):
                square_x(1, k)
            split_hi()
            for k in range(4, 8):
                square_x(1, k)
            split_hi()
            norm_scale(1)
            act.wait_ge(p_evac, tile_done("dt", GROUPS, 0))
            link(act.activation(t2[:, :], t1[:, :], ACT.Abs))
            act.activation(t2[:, :], t2[:, :], ACT.Exp, scale=-1.0).then_inc(dt_e, 1)
            act.wait_ge(dt_u, 1)
            link(act.activation(t4[:, :], t3[:, :], ACT.Ln))
            act.activation(aT[:, :], t4[:, :], ACT.Exp, scale=-1.0).then_inc(dt_ln, 1)
            split_hi()

            def silu_conv(g, i):
                k = 6 * g + i
                if i == 2 and g:
                    act.wait_ge(p_done, tile_done("out", GROUPS + g - 1, 7))
                act.wait_ge(conv_done, k + 1)
                dst = bc[:, i, :] if i < 2 else xc[:, i - 2, :]
                b = conv_bc(conv_tile(g, i))
                act.activation(dst[:, 0:PROMPT], cv[k % 2][:, 0:PROMPT], ACT.Silu, bias=b)
                act.activation(dst[:, PROMPT:T].rearrange("p (b s) -> p b s", b=DEC_B),
                               cv[k % 2][:, PROMPT + HALO:CONV_IN].rearrange("p (b s) -> p b s", s=SEG)[:, :, 0:DEC_S],
                               ACT.Silu, bias=b).then_inc(act_ready, 1)
                if i >= 2:
                    if k == 2:
                        act.wait_ge(a_ready, 1)
                    act.wait_ge(act_ready, k + 1)
                    t = 4 * g + i - 2
                    act.activation(y[:, i - 2, :], xc[:, i - 2, :], ACT.Copy,
                                   scale=dskip[:, t:t + 1]).then_inc(skip_ready, 1)

            def load_a(v):
                g, c = v // UNITS, ORDER[v % UNITS]
                n = LEN[c]
                if v % UNITS == 0:
                    act.wait_ge(hal_tr, g + 1)
                if v % UNITS == 1:
                    act.wait_ge(cn_out, 96 * (g + 1))
                if v >= 2:
                    act.wait_ge(b_done, v - 1)
                src = a_scratch[SSM_H * g:SSM_H * (g + 1), COL[c]:COL[c] + n]
                act.dma_start(seg[v % 2][0:n, :, 0:n], src.partition_broadcast(n)).then_inc(e_in[v % 2], 16)

            for g in range(GROUPS):
                s = GROUPS + g
                silu_conv(g, 0)
                silu_conv(g, 1)
                if g:
                    split_hi(2)
                silu_conv(g, 2)
                silu_conv(g, 3)
                split_hi(2)
                silu_conv(g, 4)
                if g == 0:
                    act.wait_ge(a_out, 16)
                load_a(UNITS * g)
                silu_conv(g, 5)
                act.wait_ge(cn_tr, g + 1)
                act.activation(conv_new[:, :], fT[0:27, 0:768], ACT.Copy).then_inc(cn_new, 1)
                exp_tables()
                if g == 0:
                    act.wait_ge(last_ready, 1)
                    act.activation(ealast[:, :, :].rearrange("p c h -> p (c h)"),
                                   last[:, 0:2, :].rearrange("p a b -> p (a b)")[:, 0:160], ACT.Exp)
                    act.activation(dec_s[:, :, :].rearrange("p t b -> p (t b)"), last[:, 2, :], ACT.Exp)
                    act.activation(ea_s[:, :, :].rearrange("p t b -> p (t b)"), pO[:, 0, :], ACT.Exp)
                    for n, c0, c1 in ((P, 1, 5), (16, 0, 1), (SAMPLE, 5, 6)):
                        if c1 < 6:
                            act.activation(ea[0:n, c0:c1, :], tok2[0:n, 1, c0:c1, :], ACT.Exp)
                        ins = act.activation(wend[0:n, c0:c1, :], wend[0:n, c0:c1, :], ACT.Exp)
                    ins.then_inc(dec_ready, 1)

                def decays(u):
                    c, v = ORDER[u], UNITS * g + u
                    n = LEN[c]
                    act.wait_ge(seg_done, v + 1)
                    e = seg[v % 2][0:n, :, 0:n]
                    act.activation(e, e, ACT.Relu, scale=-1.0).then_inc(clamped, 1)
                    act.wait_ge(clamped, v + 1)
                    act.activation(e, e, ACT.Exp, scale=-1.0).then_inc(l_done, 1)

                act.wait_ge(b_ready, g + 1)
                for b in range(DEC_B):
                    ins = act.activation(bmask[:, b, :], b_parts[:, :].bitcast(F32), ACT.Copy,
                                         scale=cst[0:STACK, C_BTOK + b:C_BTOK + b + 1])
                ins.then_inc(bmask_ready, 1)
                for b in range(DEC_B):
                    if b == 4:
                        load_a(UNITS * g + 1)
                        decays(0)
                    w = DEC_B * g + b
                    act.wait_ge(str_done, w + 1)
                    if w >= 2:
                        act.wait_ge(yo_done, w - 1)
                    if b == 0 and g:
                        act.wait_ge(fs_out, 16 * g)
                    act.activation(sT[b % 2][:, :], pO[:, b % 2, :], ACT.Copy).then_inc(sT_ready, 1)
                split_hi()
                for u in range(1, UNITS):
                    decays(u)
                    if u + 1 < UNITS:
                        load_a(UNITS * g + u + 1)
                    if u == 3:
                        split_hi()
                for t in range(HEADS):
                    act.wait_ge(p_evac, tile_done("z", s, t))
                    act.activation(z[:, t, :], z[:, t, :], ACT.Silu).then_inc(silu_ready, 1)
                def square_y(part):
                    for t in range(HEADS):
                        act.wait_ge(yz_ready, 8 * g + 4 * part + t + 1)
                        act.activation(xc[:, t, part_of(part)], z[:, t, part_of(part)], ACT.Square).then_inc(sqy_ready, 1)

                def scale_y(part):
                    act.wait_ge(ssy_done, 2 * g + part + 1)
                    v = rg[:, part_of(part)]
                    n = T - EARLY if part else EARLY
                    link(act.activation(v, pS[:, part, 0:n], ACT.Ln, bias=eps[:, 0:1], scale=1.0 / WIDTH))
                    act.activation(v, v, ACT.Exp, scale=-0.5).then_inc(rg_ready, 1)

                def high_y(part):
                    for t in range(HEADS):
                        act.wait_ge(yn_ready, 8 * g + 4 * part + t + 1)
                        act.activation(y_hi[:, t, part_of(part)], z[:, t, part_of(part)], ACT.Copy).then_inc(og_hi, 1)

                square_y(0)
                exp_tables()
                scale_y(0)
                square_y(1)
                if g + 1 < GROUPS:
                    split_hi()
                high_y(0)
                scale_y(1)
                high_y(1)
                act.wait_ge(fs_tr, g + 1)
                act.activation(sT[0][:, :], pS[:, 1, :], ACT.Copy).then_inc(fs_ready, 1)
            assert done[0] == len(slabs), (done[0], len(slabs))
            for t in range(KM):
                act.wait_ge(yt_done, t + 1)
                if t >= 2:
                    act.wait_ge(y_out[t % 2], 32 * (t // 2))
                src = fS if t % 2 == 0 else fT
                act.activation(yout[t % 2][:, 0:4, :].rearrange("p c d -> p (c d)"), src[:, 0:512], ACT.Copy)
                act.activation(yout[t % 2][0:32, 4, :], src[0:32, 512:640], ACT.Copy).then_inc(yout_ready, 1)

        @block.tensor
        def _(pe):
            def project(kind, s, tile, half):
                j = half_no[(kind, s, tile, half)]
                per = per_slab[kind]
                n = slab_no[(kind, s, tile // per)]
                if tile % per == 0 and half == 0:
                    pe.wait_ge(w_hi, n + 1)
                    pe.wait_ge(w_lo, n + 1)
                if j >= 2:
                    pe.wait_ge(p_evac, j - 1)
                hi = slab_view(w_hi_buf[n % HI_SLOTS], kind)
                lo = slab_view(w_lo_buf[n % LO_SLOTS], kind)
                cols = slice((tile % per) * P, (tile % per + 1) * P)
                tk = slice(half * HALF, (half + 1) * HALF)
                if kind == "out":
                    depth = HEADS
                    a_hi, a_lo = (og_hi1, og_lo1) if s < GROUPS else (y_hi, y_lo)
                else:
                    depth = KM
                    a_hi, a_lo = h_hi, h_lo
                dst = pp[:, j % 2, 0:HALF]
                for k in range(depth):
                    if kind == "out":
                        if tile == 0 and (half == 0 or s >= GROUPS):
                            done = 4 * s if s < GROUPS else 4 * GROUPS + 8 * (s - GROUPS) + 4 * half
                            pe.wait_ge(og_hi, done + k + 1)
                            pe.wait_ge(og_lo, done + k + 1)
                    elif (kind, s) in (("kv", 0), ("dt", GROUPS)) and tile == 0 and half == 0:
                        pe.wait_ge(h_ready, (s // GROUPS) * KM + k + 1)
                    pe.matmul(dst, hi[:, k, cols], a_hi[:, k, tk], start=(k == 0), stop=False)
                    pe.matmul(dst, hi[:, k, cols], a_lo[:, k, tk], start=False, stop=False)
                    mm = pe.matmul(dst, lo[:, k, cols], a_hi[:, k, tk], start=False, stop=(k == depth - 1))
                mm.then_inc(p_done, 1)

            def tile_of(kind, s, tile):
                for half in range(2):
                    project(kind, s, tile, half)

            def sum_x(k):
                pe.wait_ge(sqx_ready, k + 1)
                for half in range(2):
                    mm = pe.matmul(pO[:, half, 0:HALF], ones[:, :], sqx[k % 2][:, half * HALF:(half + 1) * HALF],
                                   start=(k == 0), stop=(k == KM - 1))
                mm.then_inc(ssx_done, 1)

            pe.wait_ge(s_ident, 16)
            pe.wait_ge(s_x[0], 48)
            pe.wait_ge(ones_ready, 3)
            for k in range(KM):
                dst = fS if k % 2 == 0 else fT
                if k == KM // 2:
                    pe.wait_ge(s_x[1], 48)
                if k >= 2:
                    pe.wait_ge(x_ready, 2 * (k - 1))
                for c in range(6):
                    n = LEN[c]
                    r = {0: 4, 5: 5}.get(c, c - 1)
                    d0 = COL[c] if c < 4 else COL[c] - 400 + 512
                    mm = pe.transpose(dst[:, d0:d0 + n], xtok[0:n, r, k * P:(k + 1) * P], ident[0:n, 0:n])
                mm.then_inc(x_tr, 1)
                if k == 1:
                    pe.wait_ge(s_par, 96)
                    pe.transpose(misc[:, 0:122], partok[0:122, 0, :], ident[0:122, 0:122])
                    pe.transpose(misc[:, 128:160], partok[0:32, 1, :], ident[0:32, 0:32]).then_inc(par_tr, 1)
                if k == 2:
                    pe.wait_ge(par_ready, 2)
                if k >= 2:
                    sum_x(k - 2)
            sum_x(KM - 2)
            sum_x(KM - 1)

            def sum_q(s, h):
                pe.wait_ge(sq_ready, 4 * s + h + 1)
                src = sq[h % 2]
                for c in range(1, 5):
                    pe.matmul(misc[:, colsum(c) + h:colsum(c) + h + 1], src[:, COL[c]:COL[c] + P],
                              ones[:, 0:1], start=True, stop=True)
                pe.matmul(misc[0:16, 17 + h:18 + h], src[:, 0:16], ones[:, 0:1], start=True, stop=True)
                pe.matmul(misc[32 * h:32 * h + 32, 16:17], src[:, PROMPT:T], ones[:, 0:1],
                          start=True, stop=True).then_inc(ssq_done, 1)

            def scores(s, u):
                c, v = ORDER[u], UNITS * s + u
                n = LEN[c]
                if u == 0:
                    pe.wait_ge(k_ready, s + 1)
                    pe.wait_ge(p_evac, tile_done("q", s, 3))
                    pe.wait_ge(kct_ready, s + 1)
                if v:
                    pe.wait_ge(soft_a, v)
                if c == 5:
                    lhs = qs[:, :]
                    pe.wait_ge(qs_ready, s + 1)
                    for i in range(2):
                        pe.matmul(pS[:, i, :], lhs, kcT[:, 4 * i:4 * i + 4, :], start=True, stop=True)
                    pe.wait_ge(c_ready, s + 1)
                    pe.matmul(misc[:, 32:64], lhs, kq[:, PROMPT:T], start=True, stop=True).then_inc(s_done, 1)
                    return
                k0, nk, _ = keys_of(c)
                for h in range(HEADS):
                    mm = pe.matmul(fS[0:n, h * 256:h * 256 + nk], q[:, h, COL[c]:COL[c] + n], kq[:, k0:k0 + nk],
                                   start=True, stop=True)
                mm.then_inc(s_done, 1)

            def transposes(s, u):
                c, v = ORDER[u], UNITS * s + u
                n = LEN[c]
                pe.wait_ge(p_ready, v + 1)
                if v:
                    pe.wait_ge(pt_ready, v)
                if u == 0:
                    pe.wait_ge(tok_ready, s + 1)
                p = sm[v % 2]
                if c == 5:
                    for b in range(DEC_B):
                        pe.transpose(fT[:, b * P:(b + 1) * P], p[:, b * P:(b + 1) * P], ident)
                    mm = pe.transpose(misc[0:32, 64:192], p[:, 1024:1056], ident)
                elif c == 0:
                    for h in range(HEADS):
                        mm = pe.transpose(fT[0:16, h * 16:h * 16 + 16], p[0:16, h * 256:h * 256 + 16], ident[0:16, 0:16])
                else:
                    first = keys_of(c)[1] - P
                    for h in range(HEADS):
                        pe.transpose(fT[0:first, h * P:(h + 1) * P], p[:, h * 256:h * 256 + first], ident)
                        mm = pe.transpose(fT[:, 512 + h * P:512 + (h + 1) * P],
                                          p[:, h * 256 + first:h * 256 + first + P], ident)
                mm.then_inc(t_done, 1)

            def values(s, u):
                c, v = ORDER[u], UNITS * s + u
                pe.wait_ge(pt_ready, v + 1)
                if v:
                    pe.wait_ge(o_ready, v)
                if u == 0:
                    pe.wait_ge(vc_in, 16 * (s + 1))
                if c == 5:
                    dst = pO[:, 0, 0:P]
                    for b in range(DEC_B):
                        pe.matmul(dst, vc[:, b, :], pT[:, b * P:(b + 1) * P], start=(b == 0), stop=False)
                    mm = pe.matmul(dst, tok[0:32, 5, :], pT[0:32, 1024:1152], start=False, stop=True)
                elif c == 0:
                    mm = pe.matmul(pO[:, 0, 0:64], tok[0:16, 4, :], pT[0:16, 0:64], start=True, stop=True)
                else:
                    first = keys_of(c)[1] - P
                    v0 = tok[0:16, 4, :] if c == 1 else tok[:, c - 2, :]
                    pe.matmul(pO[:, 0, :], v0, pT[0:first, 0:512], start=True, stop=False)
                    mm = pe.matmul(pO[:, 0, :], tok[:, c - 1, :], pT[:, 512:1024], start=False, stop=True)
                mm.then_inc(pv_done, 1)

            for s in range(GROUPS):
                if s == 0:
                    tile_of("kv", s, 0)
                tile_of("kv", s, 1)
                if s:
                    for t in range(8):
                        tile_of("out", s - 1, t)
                pe.wait_ge(ksq_ready, s + 1)
                if s:
                    pe.wait_ge(soft_a, UNITS * s)
                else:
                    pe.wait_ge(x_ready, 2 * KM)
                for half in range(2):
                    mm = pe.matmul(pS[:, half, 0:HALF], ones[:, :], ksq[:, half * HALF:(half + 1) * HALF],
                                   start=True, stop=True)
                mm.then_inc(kss_done, 1)
                pe.wait_ge(kc_in, 16 * (s + 1))
                if s:
                    pe.wait_ge(pt_ready, UNITS * s)
                for b in range(DEC_B):
                    mm = pe.transpose(fT[:, b * P:(b + 1) * P], kc[:, b, :], ident)
                mm.then_inc(kct_tr, 1)
                tile_of("q", s, 0)
                tile_of("q", s, 1)
                pe.wait_ge(k_ready, s + 1)
                pe.wait_ge(kct_ready, s + 1)
                for c in range(1, 5):
                    pe.transpose(fT[:, (c - 1) * P:c * P], vT[:, COL[c]:COL[c] + P], ident)
                pe.transpose(fT[0:16, 512:640], vT[:, 0:16], ident)
                pe.transpose(fT[0:32, 640:768], vT[:, PROMPT:T], ident)
                pe.transpose(fT[:, 768:896], kT[:, COL[4]:COL[4] + P], ident)
                pe.transpose(fT[0:32, 896:1024], kT[:, PROMPT:T], ident).then_inc(tok_tr, 1)
                if s == 0:
                    pe.wait_ge(rs_ready, 1)
                sum_q(s, 0)
                tile_of("q", s, 2)
                sum_q(s, 1)
                tile_of("q", s, 3)
                sum_q(s, 2)
                project("gate", s, 0, 0)
                sum_q(s, 3)
                scores(s, 0)
                project("gate", s, 0, 1)
                rest = [(t, half) for t in range(1, 4) for half in range(2)]
                for u in range(1, UNITS):
                    scores(s, u)
                    if u == 1:
                        project("gate", s, *rest.pop(0))
                    transposes(s, u - 1)
                    project("gate", s, *rest.pop(0))
                    values(s, u - 1)
                if s + 1 < GROUPS:
                    project("kv", s + 1, 0, 0)
                transposes(s, UNITS - 1)
                if s + 1 < GROUPS:
                    project("kv", s + 1, 0, 1)
                values(s, UNITS - 1)
            for t in range(8):
                tile_of("out", GROUPS - 1, t)
            project("dt", GROUPS, 0, 0)
            pe.wait_ge(sx_ready, KM - 1)
            for half in range(2):
                mm = pe.matmul(pO[:, half, 0:HALF], ones[:, :], xsum[:, half * HALF:(half + 1) * HALF],
                               start=True, stop=True)
            mm.then_inc(ssx_done, 1)
            project("dt", GROUPS, 0, 1)

            def part_a(g, u):
                c, v = ORDER[u], UNITS * g + u
                n = LEN[c]
                cols = slice(COL[c], COL[c] + n)
                if u == 0:
                    pe.wait_ge(act_ready, 6 * (g + 1))
                    if g:
                        pe.wait_ge(fs_ready, g)
                if v:
                    pe.wait_ge(xw_done, v)
                if u == 1:
                    pe.wait_ge(sn_done, DEC_B * (g + 1))
                pe.matmul(pS[0:n, 0, 0:n], bc[:, 0, cols], bc[:, 1, cols], start=True, stop=True)
                pe.transpose(pS[0:n, 0, P:2 * P], bc[:, 0, cols], ident)
                for t in range(HEADS):
                    mm = pe.transpose(pS[0:n, 1, t * P:(t + 1) * P], xc[:, t, cols], ident)
                mm.then_inc(a_done, 1)

            def start_states(g, fill):
                def y_of(b):
                    pe.wait_ge(sT_ready, DEC_B * g + b + 1)
                    c0 = PROMPT + b * DEC_S
                    for t in range(HEADS):
                        mm = pe.matmul(pT_[:, 1, t * SAMPLE + b * DEC_S:t * SAMPLE + (b + 1) * DEC_S],
                                       sT[b % 2][:, t * P:(t + 1) * P], bc[:, 1, c0:c0 + DEC_S], start=True, stop=True)
                    mm.then_inc(yo_done, 1)

                pe.wait_ge(cn_new, g + 1)
                for pair in range(DEC_B // 2):
                    for b in (2 * pair, 2 * pair + 1):
                        w = DEC_B * g + b
                        pe.wait_ge(sn_in[w % STATE_SLOTS], 16 * (w // STATE_SLOTS + 1))
                        if b >= 2:
                            pe.wait_ge(sT_ready, w - 1)
                        elif g == 0:
                            pe.wait_ge(dec_ready, 1)
                        else:
                            pe.wait_ge(d_done, UNITS * g)
                            pe.wait_ge(st_done, 5 * g)
                        for t in range(HEADS):
                            mm = pe.transpose(pO[:, b % 2, t * P:(t + 1) * P], s_in[w % STATE_SLOTS][:, t, :], ident)
                        mm.then_inc(str_done, 1)
                    for i in range(2):
                        if pair:
                            pe.wait_ge(sn_done, DEC_B * g + 2 * pair + i - 1)
                        else:
                            pe.wait_ge(xw_done, UNITS * g + 1)
                            pe.wait_ge(bmask_ready, g + 1)
                        for t in (2 * i, 2 * i + 1):
                            mm = pe.matmul(pS[:, i, (t % 2) * 256:(t % 2 + 1) * 256], x_parts[:, t * P:(t + 1) * P],
                                           bmask[:, 2 * pair:2 * pair + 2, :], start=True, stop=True)
                        mm.then_inc(outer_done, 1)
                    if pair in fill:
                        project("z", GROUPS + g, *fill[pair])
                    y_of(2 * pair)
                    y_of(2 * pair + 1)

            def part_b(g, u):
                c, v = ORDER[u], UNITS * g + u
                n = LEN[c]
                cols = slice(COL[c], COL[c] + n)
                pe.wait_ge(m_done, v + 1)
                pe.wait_ge(xw_done, v + 1)
                if v:
                    pe.wait_ge(y_done, v)
                for e in range(SSM_H):
                    mm = pe.matmul(pT_[0:n, 0, e * 64:(e + 1) * 64], seg[v % 2][0:n, e, 0:n],
                                   xdt[0:n, v % 2, e * 64:(e + 1) * 64], start=True, stop=True)
                if c == 5:
                    mm.then_inc(b_done, 1)
                    return
                if c:
                    pe.wait_ge(st_done, 5 * g + u - 1)
                    pe.matmul(pT_[0:n, 1, :], bc[:, 1, cols], state[:, :], start=True, stop=True)
                if u == 1:
                    pe.wait_ge(sT_ready, DEC_B * (g + 1))
                pe.matmul(pO[:, 0, :], btok[0:n, v % 2, :], xw[0:n, v % 2, :], start=True, stop=True).then_inc(b_done, 1)

            def part_c(g, u):
                c, v = ORDER[u], UNITS * g + u
                n = LEN[c]
                pe.wait_ge(y_done, v + 1)
                if u == 0:
                    pe.wait_ge(sT_ready, DEC_B * (g + 1))
                if v:
                    pe.wait_ge(d_done, v)
                for t in range(HEADS):
                    mm = pe.transpose(pO[:, 1, t * P:t * P + n], ytok[0:n, t * P:(t + 1) * P], ident[0:n, 0:n])
                mm.then_inc(c_done, 1)

            def sum_y(g, part):
                tk = part_of(part)
                for t in range(HEADS):
                    pe.wait_ge(sqy_ready, 8 * g + 4 * part + t + 1)
                    mm = pe.matmul(pS[:, part, 0:T - EARLY if part else EARLY], ones[:, :], xc[:, t, tk],
                                   start=(t == 0), stop=(t == HEADS - 1))
                mm.then_inc(ssy_done, 1)

            def final_state(g):
                pe.wait_ge(st_done, 5 * (g + 1))
                pe.wait_ge(rg_ready, 2 * (g + 1))
                for t in range(HEADS):
                    mm = pe.transpose(pS[:, 1, t * P:(t + 1) * P], state[:, t * P:(t + 1) * P], ident)
                mm.then_inc(fs_tr, 1)

            for g in range(GROUPS):
                s = GROUPS + g
                if g == 0:
                    tile_of("bc", s, 0)
                pe.wait_ge(ci_in, 48 * (g + 1))
                if g:
                    pe.wait_ge(rg_ready, 2 * g - 1)
                else:
                    pe.wait_ge(soft_a, UNITS * GROUPS)
                for i in range(6):
                    mm = pe.transpose(pS[:, 0, i * 24:(i + 1) * 24], conv_tok[:, i * P:(i + 1) * P], ident[0:24, 0:24])
                mm.then_inc(hal_tr, 1)
                if g == 0:
                    tile_of("bc", s, 1)
                project("x", s, 0, 0)
                if g:
                    sum_y(g - 1, 1)
                project("x", s, 0, 1)
                if g:
                    final_state(g - 1)
                tile_of("x", s, 1)
                if g:
                    for t in range(8):
                        tile_of("out", s - 1, t)
                project("x", s, 2, 0)
                if g == 0:
                    pe.wait_ge(a_ready, 1)
                    for i, src in enumerate((dtT, aT)):
                        for c in range(6):
                            mm = pe.transpose(pS[0:LEN[c], 1, i * 192 + c * 32:i * 192 + c * 32 + 32],
                                              src[:, COL[c]:COL[c] + LEN[c]], ident[0:32, 0:32])
                    mm.then_inc(dt_tr, 1)
                project("x", s, 2, 1)
                project("x", s, 3, 0)
                if g == 0:
                    pe.wait_ge(dt_tok, 3)
                    pe.wait_ge(decin_ready, 1)
                    pe.matmul(pS[:, 1, 0:128], ident[:, P - 1:P].to_broadcast([P, P]),
                              tok2[:, 1, 1:5, :], start=True, stop=True)
                    pe.matmul(pS[:, 1, 128:160], ident[0:16, 15:16].to_broadcast([16, P]),
                              tok2[0:16, 1, 0, :], start=True, stop=True)
                    pe.matmul(pS[0:32, 1, 160:192], cst[0:32, C_LAST:C_LAST + 32], tok2[0:32, 1, 5, :],
                              start=True, stop=True)
                    pe.wait_ge(rs_ready, 2)
                    for i in range(2):
                        pe.matmul(pO[64 * i:64 * i + 64, 0, :], ones[0:32, 0:64], ea_in[:, i, :, :],
                                  start=True, stop=True)
                    for i in range(2):
                        mm = pe.matmul(pS[64 * i:64 * i + 64, 1, 256:384], ones[0:32, 0:64],
                                       dec_in[:, i, :, :], start=True, stop=True)
                    mm.then_inc(last_done, 1)
                project("x", s, 3, 1)
                part = [(t, half) for t in range(4) for half in range(2)]
                project("z", s, *part.pop(0))
                pe.wait_ge(conv_done, 6 * (g + 1))
                if g:
                    pe.wait_ge(d_done, UNITS * g)
                else:
                    pe.wait_ge(pt_ready, UNITS * GROUPS)
                for i in range(6):
                    mm = pe.transpose(fT[0:27, i * P:(i + 1) * P], cn[:, i, :], ident)
                mm.then_inc(cn_tr, 1)
                part_a(g, 0)
                project("z", s, *part.pop(0))
                start_states(g, {pair: part.pop(0) for pair in fill_pairs(g)})
                part_b(g, 0)
                part_a(g, 1)
                part_c(g, 0)
                project("z", s, *part.pop(0))
                for u in range(2, UNITS):
                    part_a(g, u)
                    part_b(g, u - 1)
                    if part:
                        project("z", s, *part.pop(0))
                    elif g + 1 < GROUPS:
                        project("bc", s + 1, 0, u - 4)
                    part_c(g, u - 1)
                if g + 1 < GROUPS:
                    project("bc", s + 1, 1, 0)
                part_b(g, UNITS - 1)
                sum_y(g, 0)
                if g + 1 < GROUPS:
                    project("bc", s + 1, 1, 1)
                part_c(g, UNITS - 1)
            sum_y(GROUPS - 1, 1)

            def result(t):
                pe.wait_ge(p_evac, tile_done("out", STAGES - 1, t))
                dst = fS if t % 2 == 0 else fT
                if t == 0:
                    pe.wait_ge(fs_ready, GROUPS)
                if t == 1:
                    pe.wait_ge(d_done, UNITS * GROUPS)
                if t >= 2:
                    pe.wait_ge(yout_ready, t - 1)
                for c in range(1, 5):
                    pe.transpose(dst[:, (c - 1) * P:c * P], x[:, t, COL[c]:COL[c] + P], ident)
                pe.transpose(dst[0:32, 512:640], x[:, t, PROMPT:T], ident).then_inc(yt_done, 1)

            for t in range(8):
                tile_of("out", STAGES - 1, t)
                if t:
                    result(t - 1)
                else:
                    final_state(GROUPS - 1)
            result(7)

        @block.vector
        def _(dve):
            steps = [0]

            def link(ins):
                steps[0] += 1
                ins.then_inc(dve_step, 1)
                dve.wait_ge(dve_step, steps[0])

            def split_x(layer, k):
                link(dve.tensor_scalar(h_hi[:, k, :], x[:, k, :], norm_c(layer, k), None, ALU.mult))
                dve.scalar_tensor_tensor(h_lo[:, k, :], x[:, k, :], norm_c(layer, k),
                                         h_hi[:, k, :].bitcast(F32), ALU.mult, ALU.subtract).then_inc(h_ready, 1)

            def bank(kind, s, tile, half):
                j = half_no[(kind, s, tile, half)]
                dve.wait_ge(p_done, j + 1)
                return pp[:, j % 2, 0:HALF]

            def scaled(dst, kind, s, tile, parts=(0, 1)):
                for half in parts:
                    tk = slice(half * HALF, (half + 1) * HALF)
                    dve.tensor_tensor(dst[:, tk], bank(kind, s, tile, half), rs[:, tk],
                                      ALU.mult).then_inc(p_evac, 1)

            def add_out(s, tile):
                for half in range(2):
                    tk = slice(half * HALF, (half + 1) * HALF)
                    dve.tensor_tensor(x[:, tile, tk], x[:, tile, tk], bank("out", s, tile, half),
                                      ALU.add).then_inc(p_evac, 1)

            dve.wait_ge(par_ready, 2)
            for k in range(KM):
                dve.wait_ge(x_ready, 2 * (k + 1))
                split_x(0, k)
            dve.wait_ge(rs_ready, 1)

            def soft_max(s, u):
                c, v = ORDER[u], UNITS * s + u
                n, cc, b = rows_of(c), colsum(c), v % 2
                dve.wait_ge(s_done, v + 1)
                dve.wait_ge(c_ready, s + 1)
                if v >= 2:
                    dve.wait_ge(t_done, v - 1)
                if c == 5:
                    dve.tensor_tensor_reduce(sm[b][:, 0:1024], fS, cst[:, C_SATT:C_SATT + 1024], 1.0, 2 * NEG,
                                             ALU.add, ALU.max, mx[:, b, 0:1])
                    link(dve.tensor_tensor_reduce(sm[b][:, 1024:1056], misc[:, 32:64],
                                                  cst[:, C_SATT + 1024:C_SATT + 1056], 1.0, 2 * NEG,
                                                  ALU.add, ALU.max, mx[:, b, 1:2]))
                    w = 1
                    link(dve.tensor_tensor(mx[:, b, 0:1], mx[:, b, 0:1], mx[:, b, 1:2], ALU.max))
                    sink = sink_rows[:, s:s + 1]
                else:
                    _, nk, m0 = keys_of(c)
                    for h in range(HEADS):
                        ins = dve.tensor_tensor_reduce(sm[b][0:n, h * 256:h * 256 + nk], fS[0:n, h * 256:h * 256 + nk],
                                                       cst[0:n, C_MASK + m0:C_MASK + m0 + nk], 1.0, 2 * NEG,
                                                       ALU.add, ALU.max, mx[0:n, b, h:h + 1])
                    link(ins)
                    w = 4
                    sink = sinks[0:n, 4 * s:4 * s + 4]
                link(dve.tensor_tensor(mxc[0:n, 0:w], mx[0:n, b, 0:w], crow[0:n, cc:cc + w], ALU.mult))
                link(dve.tensor_tensor(msk[0:n, 0:w], mxc[0:n, 0:w], sink, ALU.max))
                dve.tensor_scalar(nm[0:n, b, 0:w], msk[0:n, 0:w], -1.0, None, ALU.mult)
                dve.tensor_tensor(ds[0:n, b, 0:w], sink, msk[0:n, 0:w], ALU.subtract).then_inc(soft_a, 1)

            def normalise(s, u):
                c, v = ORDER[u], UNITS * s + u
                n, b = rows_of(c), v % 2
                w = 1 if c == 5 else 4
                dve.wait_ge(exp_done, v + 1)
                link(dve.tensor_tensor(dsum[0:n, 0:w], den[0:n, b, 0:w], es[0:n, b, 0:w], ALU.add))
                link(dve.reciprocal(rden[0:n, 0:w], dsum[0:n, 0:w]))
                for h in range(w):
                    p = sm[b][:, :] if c == 5 else sm[b][0:n, h * 256:h * 256 + keys_of(c)[1]]
                    ins = dve.tensor_scalar(p, p, rden[0:n, h:h + 1], None, ALU.mult)
                ins.then_inc(p_ready, 1)

            dve.wait_ge(s_small, 16 * 9)
            dve.wait_ge(s_const, 16)
            for s in range(GROUPS):
                if s == 0:
                    scaled(kn, "kv", s, 0)
                scaled(vT, "kv", s, 1, (1,) if s else (0, 1))
                if s:
                    for t in range(8):
                        add_out(s - 1, t)
                dve.wait_ge(rk_ready, s + 1)
                link(dve.scalar_tensor_tensor(kT[:, :], kn[:, :], kw, rk[:, :], ALU.mult, ALU.mult))
                dve.tensor_scalar(kq[:, :], kT[:, :], qw, None, ALU.mult).then_inc(k_ready, 1)
                for h in range(HEADS):
                    scaled(q[:, h, :], "q", s, h)
                dve.wait_ge(p_evac, tile_done("q", s, 3))
                dve.tensor_copy(qs[:, :].rearrange("p (h t) -> p h t", h=HEADS), q[:, :, PROMPT:T]).then_inc(qs_ready, 1)
                rest = [(t, half) for t in range(4) for half in range(2)]

                def evac_gate():
                    t, half = rest.pop(0)
                    tk = slice(half * HALF, (half + 1) * HALF)
                    dve.tensor_tensor(gate[:, t, tk], bank("gate", s, t, half), rs[:, tk],
                                      ALU.mult).then_inc(p_evac, 1)

                if s:
                    dve.wait_ge(og_hi, 4 * s)
                evac_gate()
                soft_max(s, 0)
                evac_gate()
                for u in range(1, UNITS):
                    normalise(s, u - 1)
                    soft_max(s, u)
                    if u == 1:
                        evac_gate()
                    evac_gate()
                if s + 1 < GROUPS:
                    dve.wait_ge(ksq_ready, s + 1)
                    normalise(s, UNITS - 1)
                    scaled(kn, "kv", s + 1, 0)
                else:
                    normalise(s, UNITS - 1)
                dve.wait_ge(o_ready, UNITS * (s + 1))
                for h in range(HEADS + 1):
                    if h == HEADS - 1 and s + 1 < GROUPS:
                        scaled(vT, "kv", s + 1, 1, (0,))
                    if h < HEADS:
                        dve.wait_ge(silu_ready, 4 * s + h + 1)
                        dve.tensor_tensor(gate[:, h, :], gate[:, h, :], o[:, h, :], ALU.mult).then_inc(og_ready, 1)
                    if h:
                        dve.wait_ge(og_hi, 4 * s + h)
                        dve.wait_ge(og_ready, 4 * s + h)
                        dve.tensor_tensor(og_lo1[:, h - 1, :], gate[:, h - 1, :], og_hi1[:, h - 1, :].bitcast(F32),
                                          ALU.subtract).then_inc(og_lo, 1)
            for t in range(8):
                add_out(GROUPS - 1, t)
                dve.wait_ge(p_evac, tile_done("out", GROUPS - 1, t))
                split_x(1, t)

            for k in (KM - 2, KM - 1):
                dve.wait_ge(sqx_ready, KM + k + 1)
                dve.wait_ge(sx_ready, k - 1)
                dve.tensor_tensor(xsum[:, :], xsum[:, :], sqx[k % 2][:, :], ALU.add).then_inc(sx_ready, 1)

            dve.wait_ge(rs_ready, 2)
            dve.memset(rb[0][:, 0:HALO], 0.0)
            dve.memset(rb[1][:, 0:HALO], 0.0)
            link(dve.memset(rb[2][:, 0:HALO], 0.0))
            dve.wait_ge(p_done, tile_done("dt", GROUPS, 0))
            for half in range(2):
                tk = slice(half * HALF, (half + 1) * HALF)
                link(dve.tensor_tensor(t1[:, tk], bank("dt", GROUPS, 0, half)[0:32], rs[0:32, tk], ALU.mult))
                dve.tensor_scalar(t1[:, tk], t1[:, tk], dtb[:, :], None, ALU.add).then_inc(p_evac, 1)

            def dt_first():
                dve.wait_ge(dt_e, 1)
                link(dve.tensor_scalar(t3[:, :], t2[:, :], 1.0, None, ALU.add))
                dve.tensor_scalar(dtT[:, :], t3[:, :], -1.0, None, ALU.add).then_inc(dt_u, 1)

            def dt_second():
                dve.wait_ge(dt_u, 1)
                link(dve.tensor_tensor(dtT[:, :], t2[:, :], dtT[:, :], ALU.subtract))
                dve.wait_ge(dt_ln, 1)
                link(dve.tensor_tensor(dtT[:, :], dtT[:, :], aT[:, :], ALU.mult))

            def dt_third():
                link(dve.tensor_tensor(dtT[:, :], dtT[:, :], t4[:, :], ALU.add))
                link(dve.scalar_tensor_tensor(dtT[:, :], t1[:, :], 0.0, dtT[:, :], ALU.max, ALU.add))
                dve.wait_ge(neg_a, 1)
                link(dve.tensor_scalar(t1[:, :], dtT[:, :], aneg[:, :], None, ALU.mult))
                dve.tensor_tensor_scan(aT[:, :], cst[0:32, C_RESET:C_RESET + T], t1[:, :], 0.0,
                                       ALU.mult, ALU.add).then_inc(a_ready, 1)

            def conv_in(g, i, half):
                r = rb[i % 3]
                kind, tile = ("bc", i) if i < 2 else ("x", i - 2)
                new = r[:, HALO + PROMPT:CONV_IN].rearrange("p (b s) -> p b s", s=SEG)
                b = bank(kind, GROUPS + g, tile, half)
                if half == 0:
                    if 6 * g + i >= 3:
                        dve.wait_ge(conv_done, 6 * g + i - 2)
                    dve.tensor_tensor(r[:, HALO:HALO + HALF], b, rs[:, 0:HALF], ALU.mult).then_inc(p_evac, 1)
                    return
                m = PROMPT - HALF
                dve.tensor_tensor(r[:, HALO + HALF:HALO + PROMPT], b[:, 0:m], rs[:, HALF:PROMPT], ALU.mult)
                dve.tensor_tensor(new[:, :, HALO:SEG], b[:, m:HALF].rearrange("p (b s) -> p b s", b=DEC_B),
                                  rs[:, PROMPT:T].rearrange("p (b s) -> p b s", b=DEC_B),
                                  ALU.mult).then_inc(p_evac, 1)

            def conv_tap(g, i, tap):
                k = 6 * g + i
                r, w, ct = rb[i % 3], cv[k % 2], conv_tile(g, i)
                if tap == 0:
                    new = r[:, HALO + PROMPT:CONV_IN].rearrange("p (b s) -> p b s", s=SEG)
                    dve.wait_ge(hal_tr, g + 1)
                    at_ = [4, 5][i] if i < 2 else i - 2
                    link(dve.tensor_copy(new[:, :, 0:HALO], pS[:, 0, at_ * 24:(at_ + 1) * 24].rearrange(
                        "p (b s) -> p b s", b=DEC_B)))
                    if k >= 2:
                        dve.wait_ge(act_ready, k - 1)
                    if i == 0 and g:
                        dve.wait_ge(cn_tr, g)
                    dve.tensor_copy(cn[:, at_, 0:HALO], r[:, PROMPT:PROMPT + HALO])
                    dve.tensor_copy(cn[:, at_, HALO:27].rearrange("p (b s) -> p b s", b=DEC_B), new[:, :, DEC_S:SEG])
                    link(dve.tensor_scalar(w[:, 0:CONV_OUT], r[:, 0:CONV_OUT], conv_wc(0, ct), None, ALU.mult))
                    return
                ins = dve.scalar_tensor_tensor(w[:, 0:CONV_OUT], r[:, tap:tap + CONV_OUT], conv_wc(tap, ct),
                                               w[:, 0:CONV_OUT], ALU.mult, ALU.add)
                if tap < 3:
                    link(ins)
                else:
                    ins.then_inc(conv_done, 1)

            def conv_taps(g, i):
                for tap in range(4):
                    conv_tap(g, i, tap)

            def conv_last(g):
                i, k = 5, 6 * g + 5
                r, w, ct = rb[i % 3], cv[k % 2], conv_tile(g, i)
                new = r[:, HALO + PROMPT:CONV_IN].rearrange("p (b s) -> p b s", s=SEG)

                def taps(c0, c1):
                    ins = dve.tensor_scalar(w[:, c0:c1], r[:, c0:c1], conv_wc(0, ct), None, ALU.mult)
                    for tap in range(1, 4):
                        link(ins)
                        ins = dve.scalar_tensor_tensor(w[:, c0:c1], r[:, tap + c0:tap + c1], conv_wc(tap, ct),
                                                       w[:, c0:c1], ALU.mult, ALU.add)
                    return ins

                conv_in(g, i, 0)
                dve.wait_ge(act_ready, k - 1)
                dve.tensor_copy(new[:, :, 0:HALO], pS[:, 0, 3 * 24:4 * 24].rearrange("p (b s) -> p b s", b=DEC_B))
                dve.wait_ge(p_evac, half_no[("x", GROUPS + g, 3, 0)] + 1)
                taps(0, HALF)
                conv_in(g, i, 1)
                dve.wait_ge(p_evac, half_no[("x", GROUPS + g, 3, 1)] + 1)
                dve.tensor_copy(cn[:, 3, 0:HALO], r[:, PROMPT:PROMPT + HALO])
                dve.tensor_copy(cn[:, 3, HALO:27].rearrange("p (b s) -> p b s", b=DEC_B), new[:, :, DEC_S:SEG])
                taps(HALF, CONV_OUT).then_inc(conv_done, 1)

            def conv(g, i):
                conv_in(g, i, 0)
                conv_in(g, i, 1)
                conv_taps(g, i)

            def heads(t, n):
                return t.rearrange("p (e d) -> p e d", e=SSM_H)

            def per_head(t, n, d=64):
                return t.unsqueeze(2).to_broadcast([n, SSM_H, d])

            def prepare(g, u):
                c, v = ORDER[u], UNITS * g + u
                n, b = LEN[c], v % 2
                hs = slice(SSM_H * g, SSM_H * (g + 1))
                dve.wait_ge(a_done, v + 1)
                if v >= 2:
                    dve.wait_ge(b_done, v - 1)
                mask = cst[0:32, C_SMASK:C_SMASK + 32] if c == 5 else cst[0:n, C_CAUS:C_CAUS + n]
                if v == 0:
                    dve.wait_ge(dec_ready, 1)
                if c == 5:
                    dve.tensor_copy(b_parts[32:64, :], pS[0:n, 0, P:2 * P])
                    link(dve.tensor_copy(b_parts[0:32, :], pS[0:n, 0, P:2 * P]))
                    dve.tensor_tensor(b_parts[64:96, :], pS[0:n, 0, P:2 * P], b_parts[0:32, :].bitcast(F32),
                                      ALU.subtract).then_inc(b_ready, 1)
                    link(dve.tensor_tensor(dtw[:, :], tok2[0:n, 0, c, hs], wend[0:n, c, hs], ALU.mult))
                    link(dve.tensor_tensor(heads(xw[0:n, b, :], n), heads(pS[0:n, 1, :], n), per_head(dtw[:, :], n),
                                           ALU.mult))
                    dve.tensor_copy(x_parts[64:96, :], xw[0:n, b, :])
                    link(dve.tensor_copy(x_parts[0:32, :], xw[0:n, b, :]))
                    dve.tensor_tensor(x_parts[32:64, :], xw[0:n, b, :], x_parts[0:32, :].bitcast(F32), ALU.subtract)
                    dve.tensor_tensor(cbm[0:n, b, 0:n], pS[0:n, 0, 0:n], mask, ALU.mult)
                    dve.tensor_tensor(heads(xdt[0:n, b, :], n), heads(pS[0:n, 1, :], n),
                                      per_head(tok2[0:n, 0, c, hs], n), ALU.mult).then_inc(xw_done, 1)
                    return
                dve.tensor_tensor(cbm[0:n, b, 0:n], pS[0:n, 0, 0:n], mask, ALU.mult)
                dve.tensor_copy(btok[0:n, b, :], pS[0:n, 0, P:2 * P])
                link(dve.tensor_tensor(heads(xdt[0:n, b, :], n), heads(pS[0:n, 1, :], n),
                                       per_head(tok2[0:n, 0, c, hs], n), ALU.mult))
                dve.tensor_tensor(heads(xw[0:n, b, :], n), heads(xdt[0:n, b, :], n),
                                  per_head(wend[0:n, c, hs], n), ALU.mult).then_inc(xw_done, 1)

            def mix(g, u):
                c, v = ORDER[u], UNITS * g + u
                n = LEN[c]
                dve.wait_ge(l_done, v + 1)
                dve.wait_ge(xw_done, v + 1)
                e = seg[v % 2][0:n, :, 0:n]
                dve.tensor_tensor(e, e, cbm[0:n, v % 2, 0:n].unsqueeze(1).to_broadcast([n, SSM_H, n]),
                                  ALU.mult).then_inc(m_done, 1)

            def combine(g, u):
                c, v = ORDER[u], UNITS * g + u
                n = LEN[c]
                hs = slice(SSM_H * g, SSM_H * (g + 1))
                dve.wait_ge(b_done, v + 1)
                if v:
                    dve.wait_ge(c_done, v)
                if c in (0, 5):
                    dve.tensor_copy(ytok[0:n, :], pT_[0:n, 0, :]).then_inc(y_done, 1)
                else:
                    link(dve.tensor_tensor(heads(ytok[0:n, :], n), heads(pT_[0:n, 1, :], n),
                                           per_head(ea[0:n, c, hs], n), ALU.mult))
                    dve.tensor_tensor(ytok[0:n, :], ytok[0:n, :], pT_[0:n, 0, :], ALU.add).then_inc(y_done, 1)

            def new_state(g, u):
                c = ORDER[u]
                if c == 5:
                    return
                if c == 0:
                    if g:
                        dve.wait_ge(fs_tr, g)
                    dve.tensor_copy(state[:, :], pO[:, 0, :]).then_inc(st_done, 1)
                    return
                dve.wait_ge(decayed, 4 * g + u - 1)
                dve.tensor_tensor(state[:, :], state[:, :], pO[:, 0, :], ALU.add).then_inc(st_done, 1)

            def add_skip(g, u):
                c, v = ORDER[u], UNITS * g + u
                n = LEN[c]
                cols = slice(COL[c], COL[c] + n)
                dve.wait_ge(c_done, v + 1)
                dve.wait_ge(skip_ready, 4 * (g + 1))
                if c == 5:
                    dve.wait_ge(yo_done, DEC_B * (g + 1))
                    dve.tensor_tensor(y_start[:, :, :], pT_[:, 1, 0:P].rearrange("p (t b) -> p t b", t=HEADS),
                                      ea_s[:, 4 * g:4 * g + 4, :], ALU.mult)
                ins = dve.tensor_tensor(y[:, :, cols], y[:, :, cols],
                                        pO[:, 1, :].rearrange("p (t n) -> p t n", t=HEADS)[:, :, 0:n], ALU.add)
                if c == 5:
                    link(ins)
                    ins = dve.tensor_tensor(y[:, :, cols], y[:, :, cols], y_start[:, :, :], ALU.add)
                ins.then_inc(d_done, 1)

            def gate_y(g, part):
                dve.wait_ge(d_done, UNITS * (g + 1) - 1 + part)
                tk = part_of(part)
                for t in range(HEADS):
                    dve.wait_ge(silu_ready, 4 * (GROUPS + g) + t + 1)
                    dve.tensor_tensor(z[:, t, tk], z[:, t, tk], y[:, t, tk], ALU.mult).then_inc(yz_ready, 1)

            def norm_y(g, part):
                tk, done = part_of(part), 8 * g + 4 * part
                dve.wait_ge(rg_ready, 2 * g + part + 1)
                for t in range(HEADS):
                    dve.scalar_tensor_tensor(z[:, t, tk], z[:, t, tk], ssmn_c(4 * g + t), rg[:, tk],
                                             ALU.mult, ALU.mult).then_inc(yn_ready, 1)
                dve.wait_ge(yz_ready, done + 4)
                for t in range(HEADS):
                    dve.wait_ge(og_hi, 4 * GROUPS + done + t + 1)
                    dve.wait_ge(yn_ready, done + t + 1)
                    dve.tensor_tensor(y_lo[:, t, tk], z[:, t, tk], y_hi[:, t, tk].bitcast(F32),
                                      ALU.subtract).then_inc(og_lo, 1)

            for g in range(GROUPS):
                s = GROUPS + g
                if g == 0:
                    dt_first()
                    conv_in(g, 0, 0)
                    dt_second()
                    conv_in(g, 0, 1)
                    conv_taps(g, 0)
                    conv_in(g, 1, 0)
                    conv_in(g, 1, 1)
                    conv_taps(g, 1)
                    conv_in(g, 2, 0)
                    conv_in(g, 2, 1)
                    conv_taps(g, 2)
                    conv_in(g, 3, 0)
                else:
                    conv_tap(g, 0, 0)
                    conv_in(g, 2, 0)
                    conv_tap(g, 0, 1)
                    conv_tap(g, 0, 2)
                    conv_in(g, 2, 1)
                    norm_y(g - 1, 1)
                    conv_tap(g, 0, 3)
                    conv_in(g, 3, 0)
                    conv_tap(g, 1, 0)
                    conv_tap(g, 1, 1)
                    conv_in(g, 3, 1)
                    conv_tap(g, 1, 2)
                    conv_tap(g, 1, 3)
                if g == 0:
                    dt_third()
                    conv_in(g, 3, 1)
                    conv_taps(g, 3)
                if g:
                    for t in range(8):
                        add_out(s - 1, t)
                        conv_tap(g, 2 + t // 4, t % 4)
                if g == 0:
                    dve.wait_ge(dt_tr, 1)
                    for n, c0, c1 in ((P, 1, 5), (16, 0, 1), (SAMPLE, 5, 6)):
                        dve.tensor_copy(tok2[0:n, :, c0:c1, :], pS[0:n, 1, 0:384].rearrange(
                            "p (a c h) -> p a c h", a=2, c=6)[:, :, c0:c1, :]).then_inc(dt_tok, 1)
                    dve.wait_ge(dt_tok, 3)
                    end = cst[0:32, C_BEND:C_BEND + 8].unsqueeze(1).to_broadcast([32, 16, DEC_B])
                    for i in range(2):
                        a_s = tok2[0:32, 1, 5, :].rearrange("p (t e) -> p e t", e=2)[:, i, :]
                        dve.tensor_tensor(ea_in[:, i, :, :], a_s.unsqueeze(2).to_broadcast([32, 16, SAMPLE]),
                                          ident[0:32, 0:32].unsqueeze(1).to_broadcast([32, 16, SAMPLE]), ALU.mult)
                        ins = dve.tensor_tensor(dec_in[:, i, :, :], a_s.unsqueeze(2).to_broadcast([32, 16, DEC_B]),
                                                end, ALU.mult)
                    ins.then_inc(decin_ready, 1)
                conv(g, 4)
                if g == 0:
                    dve.wait_ge(last_done, 1)
                    dve.tensor_copy(last[:, 0:2, :].rearrange("p a b -> p (a b)")[:, 0:160], pS[:, 1, 0:160])
                    dve.tensor_copy(last[0:32, 1, 32:64], pS[0:32, 1, 160:192])
                    link(dve.tensor_copy(last[:, 2, :], pS[:, 1, 256:384]))
                    dve.tensor_tensor(wend[:, 1:5, :], last[:, 0, :].rearrange("p (c h) -> p c h", c=4),
                                      tok2[:, 1, 1:5, :], ALU.subtract)
                    dve.tensor_tensor(wend[0:16, 0, :], last[0:16, 1, 0:32], tok2[0:16, 1, 0, :], ALU.subtract)
                    dve.tensor_tensor(wend[0:32, 5, :], last[0:32, 1, 32:64], tok2[0:32, 1, 5, :],
                                      ALU.subtract).then_inc(last_ready, 1)
                conv_last(g)
                part = [(t, half) for t in range(4) for half in range(2)]

                def evac_z():
                    t, half = part.pop(0)
                    tk = slice(half * HALF, (half + 1) * HALF)
                    dve.tensor_tensor(z[:, t, tk], bank("z", s, t, half), rs[:, tk], ALU.mult).then_inc(p_evac, 1)

                if g == 0:
                    dve.wait_ge(a_out, 16)
                    dve.wait_ge(dt_tr, 1)
                evac_z()
                prepare(g, 0)
                evac_z()
                for pair in range(DEC_B // 2):
                    for i in range(2):
                        dve.wait_ge(outer_done, DEC_B * g + 2 * pair + i + 1)
                        for b in (2 * pair, 2 * pair + 1):
                            for t in (2 * i, 2 * i + 1):
                                st = s_in[(DEC_B * g + b) % STATE_SLOTS][:, t, :]
                                c0 = (t % 2) * 256 + (b % 2) * P
                                ins = dve.scalar_tensor_tensor(st, st, dec_s[:, 4 * g + t, b:b + 1],
                                                               pS[:, i, c0:c0 + P], ALU.mult, ALU.add)
                        ins.then_inc(sn_done, 1)
                    if pair in fill_pairs(g):
                        evac_z()
                    if pair == 2:
                        mix(g, 0)
                combine(g, 0)
                add_skip(g, 0)
                prepare(g, 1)
                evac_z()
                mix(g, 1)
                for u in range(2, UNITS):
                    prepare(g, u)
                    combine(g, u - 1)
                    new_state(g, u - 1)
                    mix(g, u)
                    if part:
                        evac_z()
                    elif g + 1 < GROUPS:
                        conv_in(g + 1, 0, u - 4)
                    add_skip(g, u - 1)
                gate_y(g, 0)
                if g + 1 < GROUPS:
                    conv_in(g + 1, 1, 0)
                combine(g, UNITS - 1)
                new_state(g, UNITS - 1)
                if g + 1 < GROUPS:
                    conv_in(g + 1, 1, 1)
                add_skip(g, UNITS - 1)
                gate_y(g, 1)
                norm_y(g, 0)
            norm_y(GROUPS - 1, 1)
            for t in range(8):
                add_out(STAGES - 1, t)


_INS = ["x_prompt", "x_sample", "cache_k", "cache_v", "state_conv", "state_ssm", "meta_tokens", "norm_w",
        "w_attn_in", "q_norm_w", "k_norm_w", "attn_sinks", "w_attn_out", "w_ssm_in", "conv_w", "conv_b",
        "dt_bias", "a_log", "d_skip", "ssm_norm_w", "w_ssm_out"]
_OUTS = [(1, 512, 1024), (8, 4, 1024), (1, 1, 128, 4, 128), (1, 1, 128, 4, 128), (1, 1, 3, 3072),
         (1, 1, 32, 64, 128), (1, 8, 128, 4, 128), (1, 8, 128, 4, 128), (1, 8, 3, 3072), (1, 8, 32, 64, 128)]


def kernel(**inputs):
    import concourse.bacc as bacc
    from concourse.bass_utils import run_bass_kernel_spmd

    nc = bacc.Bacc("TRN2", target_bir_lowering=False, num_devices=1)
    arrays, args = {}, []
    for name in _INS + ["consts"]:
        a = np.ascontiguousarray(shape_constants() if name == "consts" else inputs[name])
        arrays[f"in_{name}"] = a
        args.append(nc.dram_tensor(f"in_{name}", a.shape, mybir.dt.from_np(a.dtype), kind="ExternalInput").ap())
    for i, shape in enumerate(_OUTS):
        args.append(nc.dram_tensor(f"out_{i}", shape, F32, kind="ExternalOutput").ap())
    args.append(nc.dram_tensor("a_scratch", (32, T), F32, kind="Internal").ap())
    build(nc, *args)
    r = run_bass_kernel_spmd(nc, [arrays], core_ids=[0])
    return tuple(r.results[0][f"out_{i}"] for i in range(len(_OUTS)))
```
